# Optimizing a Trainium2 kernel written in Bass

```python
import jax, jax.numpy as jnp
from jax import lax
import numpy as np

D_MODEL = 2048
BATCH = 1
SEQ = 256
DEPTH = 1

CHUNK = 64
N_META = 16
LEAD_PAD = CHUNK - N_META
Q_BLOCK = 128

MIX_WIDTH = D_MODEL
RET_WIDTH = MIX_WIDTH // 2
MLA_WIDTH = MIX_WIDTH - RET_WIDTH

RET_HEADS = 8
RET_HEAD_DIM = RET_WIDTH // RET_HEADS

MLA_HEADS = 8
MLA_V_DIM = MLA_WIDTH // MLA_HEADS
MLA_NOPE_DIM = 128
MLA_ROPE_DIM = 64
Q_LORA = 512
KV_LORA = 256
MLA_QK_DIM = MLA_NOPE_DIM + MLA_ROPE_DIM

D_FF = 4 * D_MODEL

ROPE_BASE = 10000.0
EPS = 1e-6

IN_SIZES = [RET_WIDTH, RET_WIDTH, RET_WIDTH, RET_WIDTH, Q_LORA, KV_LORA, MLA_ROPE_DIM]
IN_WIDTH = int(sum(IN_SIZES))
IN_SPLITS = [int(v) for v in np.cumsum(IN_SIZES)[:-1]]

kernel_name = "hymba_retention_mla_streaming_block"

def rmsnorm(x, g):
    xf = x.astype(jnp.float32)
    y = xf * lax.rsqrt(jnp.mean(xf * xf, axis=-1, keepdims=True) + EPS)
    return (y * g.astype(jnp.float32)).astype(x.dtype)

def rope_tables(pos, dim):
    inv = 1.0 / (ROPE_BASE ** (jnp.arange(0, dim, 2, dtype=jnp.float32) / dim))
    ang = pos[:, None] * inv[None, :]
    return jnp.cos(ang), jnp.sin(ang)

def apply_rope(x, cos, sin):
    half = x.shape[-1] // 2
    cos = cos.astype(x.dtype)
    sin = sin.astype(x.dtype)
    x1, x2 = x[..., :half], x[..., half:]
    return jnp.concatenate([x1 * cos - x2 * sin, x1 * sin + x2 * cos], axis=-1)

def retention_chunkwise(q, k, v):
    B, L, H, dk = q.shape
    dv = v.shape[-1]
    nc = L // CHUNK
    dt = q.dtype
    log_gamma = jnp.log(1.0 - 2.0 ** (-5.0 - jnp.arange(H, dtype=jnp.float32)))
    q = (q * (dk ** -0.5)).reshape(B, nc, CHUNK, H, dk)
    k = k.reshape(B, nc, CHUNK, H, dk)
    v = v.reshape(B, nc, CHUNK, H, dv)
    idx = jnp.arange(CHUNK, dtype=jnp.float32)
    dist = jnp.abs(idx[:, None] - idx[None, :])
    d_intra = jnp.exp(log_gamma[:, None, None] * dist[None]).astype(dt)
    scores = jnp.einsum('bnihd,bnjhd->bnhij', q, k) * d_intra
    o_intra = jnp.einsum('bnhij,bnjhe->bnihe', scores, v)
    w_k = jnp.exp(log_gamma[None, :] * (CHUNK - 1.0 - idx)[:, None]).astype(dt)
    kv = jnp.einsum('bnjhd,jh,bnjhe->bnhde', k, w_k, v)
    chunk_decay = jnp.exp(log_gamma * CHUNK).astype(kv.dtype)[None, :, None, None]

    def step(state, kv_c):
        return state * chunk_decay + kv_c, state

    _, states = lax.scan(step, jnp.zeros((B, H, dk, dv), kv.dtype), jnp.moveaxis(kv, 1, 0))
    states = jnp.moveaxis(states, 0, 1)
    w_q = jnp.exp(log_gamma[None, :] * (idx + 1.0)[:, None]).astype(dt)
    o_inter = jnp.einsum('bnihd,ih,bnhde->bnihe', q, w_q, states)
    return (o_intra + o_inter).reshape(B, L, H, dv)

def head_groupnorm(o, g):
    of = o.astype(jnp.float32)
    mu = jnp.mean(of, axis=-1, keepdims=True)
    var = jnp.mean(jnp.square(of - mu), axis=-1, keepdims=True)
    y = ((of - mu) * lax.rsqrt(var + EPS)).reshape(o.shape[0], o.shape[1], -1)
    return (y * g.astype(jnp.float32)).astype(o.dtype)

def mla_attention(q_lat, q_rope, c_kv, k_rope, chunk_id, key_valid):
    B, L, H, C = q_lat.shape
    nqb = L // Q_BLOCK
    scale = MLA_QK_DIM ** -0.5
    neg = jnp.finfo(jnp.float32).min
    ql_b = jnp.moveaxis(q_lat.reshape(B, nqb, Q_BLOCK, H, C), 1, 0)
    qr_b = jnp.moveaxis(q_rope.reshape(B, nqb, Q_BLOCK, H, q_rope.shape[-1]), 1, 0)
    qc_b = chunk_id.reshape(nqb, Q_BLOCK)

    def attend(args):
        ql, qr, qc = args
        s = (jnp.einsum('bqhc,bkc->bhqk', ql, c_kv)
             + jnp.einsum('bqhr,bkr->bhqk', qr, k_rope)).astype(jnp.float32) * scale
        mask = (chunk_id[None, :] <= qc[:, None]) & key_valid[None, :]
        s = jnp.where(mask[None, None], s, neg)
        p = jax.nn.softmax(s, axis=-1).astype(c_kv.dtype)
        return jnp.einsum('bhqk,bkc->bqhc', p, c_kv)

    o = lax.map(attend, (ql_b, qr_b, qc_b))
    return jnp.moveaxis(o, 0, 1).reshape(B, L, H, C)

def setup_inputs(seed: int = 0) -> dict:
    key = jax.random.key(seed)
    ks = jax.random.split(key, 16)
    f32 = jnp.float32

    def w(k, shape, fan_in):
        return jax.random.normal(k, shape, f32) * (fan_in ** -0.5)

    def gain(k, shape):
        return 1.0 + 0.02 * jax.random.normal(k, shape, f32)

    return {
        "x": jax.random.normal(ks[0], (BATCH, SEQ, D_MODEL), f32),
        "meta_tokens": jax.random.normal(ks[1], (N_META, D_MODEL), f32),
        "norm_mix_g": gain(ks[2], (DEPTH, D_MODEL)),
        "w_in": w(ks[3], (DEPTH, D_MODEL, IN_WIDTH), D_MODEL),
        "ret_out_g": gain(ks[4], (DEPTH, RET_WIDTH)),
        "q_norm_g": gain(ks[5], (DEPTH, Q_LORA)),
        "w_uq": w(ks[6], (DEPTH, Q_LORA, MLA_HEADS * MLA_QK_DIM), Q_LORA),
        "kv_norm_g": gain(ks[7], (DEPTH, KV_LORA)),
        "w_uk": w(ks[8], (DEPTH, KV_LORA, MLA_HEADS * MLA_NOPE_DIM), KV_LORA),
        "w_uv": w(ks[9], (DEPTH, KV_LORA, MLA_HEADS * MLA_V_DIM), KV_LORA),
        "mla_out_g": gain(ks[10], (DEPTH, MLA_WIDTH)),
        "w_o": w(ks[11], (DEPTH, MIX_WIDTH, D_MODEL), MIX_WIDTH),
        "norm_mlp_g": gain(ks[12], (DEPTH, D_MODEL)),
        "w_up": w(ks[13], (DEPTH, D_MODEL, D_FF), D_MODEL),
        "w_down": w(ks[14], (DEPTH, D_FF, D_MODEL), D_FF),
        "final_norm_g": gain(ks[15], (D_MODEL,)),
    }

def reference(x, meta_tokens, norm_mix_g, w_in, ret_out_g, q_norm_g, w_uq, kv_norm_g,
              w_uk, w_uv, mla_out_g, w_o, norm_mlp_g, w_up, w_down, final_norm_g):
    B, S, D = x.shape
    dt = x.dtype
    tail = (-(CHUNK + S)) % Q_BLOCK
    L = CHUNK + S + tail
    h = jnp.concatenate([
        jnp.zeros((B, LEAD_PAD, D), dt),
        jnp.broadcast_to(meta_tokens.astype(dt)[None], (B, N_META, D)),
        x,
        jnp.zeros((B, tail, D), dt),
    ], axis=1)

    p = jnp.arange(L)
    chunk_id = p // CHUNK
    key_valid = p >= LEAD_PAD
    valid_f = key_valid.astype(dt)[None, :, None, None]
    pos = jnp.maximum(p - LEAD_PAD, 0).astype(jnp.float32)
    cos_r, sin_r = rope_tables(pos, RET_HEAD_DIM)
    cos_m, sin_m = rope_tables(pos, MLA_ROPE_DIM)

    for l in range(DEPTH):
        u = rmsnorm(h, norm_mix_g[l])
        proj = u @ w_in[l]
        rq, rk, rv, rg, cq, ckv, kr = jnp.split(proj, IN_SPLITS, axis=-1)

        rq = apply_rope(rq.reshape(B, L, RET_HEADS, RET_HEAD_DIM), cos_r[:, None, :], sin_r[:, None, :])
        rk = apply_rope(rk.reshape(B, L, RET_HEADS, RET_HEAD_DIM), cos_r[:, None, :], sin_r[:, None, :]) * valid_f
        rv = rv.reshape(B, L, RET_HEADS, RET_HEAD_DIM)
        ret = retention_chunkwise(rq, rk, rv)
        ret_out = jax.nn.silu(rg) * head_groupnorm(ret, ret_out_g[l])

        c_q = rmsnorm(cq, q_norm_g[l])
        q = (c_q @ w_uq[l]).reshape(B, L, MLA_HEADS, MLA_QK_DIM)
        q_nope = q[..., :MLA_NOPE_DIM]
        q_rope = apply_rope(q[..., MLA_NOPE_DIM:], cos_m[:, None, :], sin_m[:, None, :])
        c_kv = rmsnorm(ckv, kv_norm_g[l])
        k_rope = apply_rope(kr, cos_m, sin_m)
        w_uk_h = w_uk[l].reshape(KV_LORA, MLA_HEADS, MLA_NOPE_DIM)
        w_uv_h = w_uv[l].reshape(KV_LORA, MLA_HEADS, MLA_V_DIM)
        q_lat = jnp.einsum('blhd,chd->blhc', q_nope, w_uk_h)
        o_lat = mla_attention(q_lat, q_rope, c_kv, k_rope, chunk_id, key_valid)
        mla = jnp.einsum('blhc,chv->blhv', o_lat, w_uv_h).reshape(B, L, MLA_WIDTH)
        mla_out = rmsnorm(mla, mla_out_g[l])

        h = h + jnp.concatenate([ret_out, mla_out], axis=-1) @ w_o[l]

        m = rmsnorm(h, norm_mlp_g[l])
        h = h + jnp.square(jax.nn.relu(m @ w_up[l])) @ w_down[l]

    return rmsnorm(h[:, CHUNK:CHUNK + S], final_norm_g)


_drawn_inputs = setup_inputs


def setup_inputs(seed=0):
    import zlib

    import numpy as np

    out = dict(_drawn_inputs(seed))
    spreads = {}
    factors = {'ret_out_g': 8.0,
     'q_norm_g': 4.841,
     'kv_norm_g': 3.386,
     'mla_out_g': 4.997,
     'norm_mlp_g': 3.66,
     'final_norm_g': 2.751}
    for name, (base, spread) in spreads.items():
        noise = np.random.default_rng([zlib.crc32(name.encode()), seed]).standard_normal(out[name].shape)
        drawn = base * np.exp(spread * noise) if base else spread * noise
        out[name] = __import__('jax').numpy.asarray(drawn.astype(out[name].dtype))
    for name, factor in factors.items():
        out[name] = (out[name] * factor).astype(out[name].dtype)
    return out
```

```python
from contextlib import ExitStack

import numpy as np

import concourse.bass as bass
from concourse import mybir

F32 = mybir.dt.float32
F32R = mybir.dt.float32r
ALU = mybir.AluOpType
ACT = mybir.ActivationFunctionType
AX = mybir.AxisListType

P = 128
D = 2048
FRAMES = 256
META = 16
TOK = META + FRAMES
CHUNK = 64
HEADS = 8
HD = 128
NOPE, ROPE = 128, 64
QL, KVL = 512, 256
DFF = 8192
EPS = 1e-6
KT = D // P
W = KT * P
RAWS = 4

C_CQ, C_KV, C_KR, C_HEAD0 = 0, 4, 6, 7
C_HEAD = C_HEAD0 + 3
C_GATE7 = C_HEAD + 4 * (HEADS - 1)
C_WO = C_GATE7 + 1
C_MLP = C_WO + KT
HALF_F = DFF // P // 2
DOWN_PER_BLOCK = HALF_F // KT
C_HALF = HALF_F + DOWN_PER_BLOCK * KT
B_HALF = HALF_F + KT
W_HEAD0 = 4
W_HEAD = 5
W_GATE7 = W_HEAD + 2 * (HEADS - 1)
W_WO = W_GATE7 + 1
W_MLP = W_WO + KT
C_END = C_MLP + 2 * C_HALF

SIDE_Q, SIDE_R, SIDE_K, SIDE_V, SIDE_END = 0, 512, 1024, 1280, 1536
K_ID, K_CEN, K_ONE, K_DIST, K_MASK, K_LG, K_COSR, K_SINR, K_COSM, K_SINM, K_EPS = (
    0, 128, 256, 384, 1024, 1440, 1448, 1720, 1992, 2264, 2536)
K_END = 2537
G_MIX, G_Q, G_KV, G_RET, G_MLA, G_MLP, G_FIN = 0, 16, 20, 22, 30, 38, 54
G_END = 70
F0, F1 = META, META + P
Q0K, Q1K = META + P, TOK
SCORES = Q0K + Q1K

EVENTS = """hi_ready lo_ready chunk_used acc_read half_b
x_hi x_lo meta_pad ssx ss_x_ps ss_q_ps ss_k_ps rx_sd rstdx rq_var cq_raw cq_sq cq_sum cq_sd cq_scaled cq_hi cq_lo
kv_raw kv_sq kv_sum kv_sd kv_scaled kv_hi kv_lo kr_raw kr_ready tables stat
side_hi side_lo qn_ps qr_ps kn_ps v_ps qn_b qr_b qn_ready qr_raw qr_ready qr_u kn_ready v_ready
mla_s_ps mla_s mla_max mla_exp mla_inv mla_p pt_ps pt_m pt_f mla_o_ps mla_o mla_sq mla_ss mla_ss_ps mla_sd
mla_rstd mla_a mla_hi mla_lo
rq_raw rq_sw rq_cos rq_sin rq_ready rk_raw rk_cos rk_sin rk_ready decay ret_s_ps ret_y_ps ret_s ret_v
ret_o_ps ret_o cen_ps cen ret_sq var_ps ret_sd ret_inv ret_y ret_a ret_hi ret_lo
gate_raw gate_z gate_exp gate_den gate_inv gate
x_back wo_res h_ready m_hi m_lo h_sq h_ss h_ss_ps h_sd h_rstd
up_z up_r up_sq up_hi up_lo dn_res dn_h dn_sq dn_ss fin_ps fin_sd fin_rstd fin_out stored
side_landed x_landed gains_landed consts_landed""".split()


def hymba_block(nc, w_in, w_side, w_o, w_up, w_down, x_all, x_frames, gains_in, consts_in, out):
    ctx = ExitStack()
    with ctx:
        sem = {n: ctx.enter_context(nc.semaphore(n)) for n in EVENTS}
        raw_landed = [ctx.enter_context(nc.semaphore(f"raw_landed{i}")) for i in range(RAWS)]
        x_part = [ctx.enter_context(nc.semaphore(f"x_part{i}")) for i in range(4)]

        at = (nc.sbuf_base + 31) // 32 * 32
        arena = ctx.enter_context(nc.sbuf_tensor("arena", [P, (nc.sbuf_usable_end - at) // 4 - 16], F32))
        here = [at]

        def place(name, shape, dt=F32):
            t = nc.alloc_sbuf_tensor_at(name, [P] + shape, dt, offset=here[0])
            size = 4
            for n in shape:
                size *= n
            here[0] += (size + 31) // 32 * 32
            return t

        raw = [place(f"raw{i}", [W]) for i in range(RAWS)]
        hi = [place(f"hi{i}", [W], F32R) for i in range(2)]
        lo = [place(f"lo{i}", [W], F32R) for i in range(2)]
        xs = place("xs", [KT, 2 * TOK], F32R)
        hid_at = here[0]
        hid = place("hid", [HALF_F, 2 * FRAMES], F32R)
        res_at = here[0]
        res = place("res", [KT, FRAMES])
        half_b = [place(f"half_b{i}", [FRAMES]) for i in range(2)]
        gains = place("gains", [G_END])
        consts = place("consts", [K_END])
        rstdx = place("rstdx", [TOK])
        sum_sq = place("sum_sq", [FRAMES])
        rstd = place("rstd", [FRAMES])
        sq = place("sq", [FRAMES])
        z = place("z", [FRAMES])
        r = place("r", [FRAMES])
        t2 = place("t2", [FRAMES])
        rest_at = here[0]

        here[0] = hid_at + 2 * KT * TOK * 4
        mla_o = place("mla_o", [HEADS, FRAMES])
        cq = place("cq", [QL // P, FRAMES])
        cqs = place("cqs", [QL // P, 2 * FRAMES], F32R)
        ckv = place("ckv", [KVL // P, TOK])
        ckvs = place("ckvs", [KVL // P, 2 * TOK], F32R)
        kr = place("kr", [TOK])
        assert here[0] <= res_at
        here[0] = hid_at + (2 * KT * TOK + HEADS * FRAMES) * 4
        decay = place("decay", [640])
        ret_v = place("ret_v", [3, P])
        here[0] = hid_at
        x_in = place("x_in", [KT, TOK])
        x_sq = place("x_sq", [KT, TOK])
        here[0] = hid_at + HEADS * 2 * FRAMES * 4
        side = place("side", [SIDE_END])
        side_hi = place("side_hi", [SIDE_V], F32R)
        zk = place("zk", [TOK])
        swk = place("swk", [TOK])
        zq = place("zq", [FRAMES])
        swq = place("swq", [FRAMES])
        rq = place("rq", [FRAMES])
        assert here[0] <= hid_at + 2 * KT * TOK * 4
        here[0] = res_at
        qn = place("qn", [FRAMES])
        qn_b = place("qn_b", [FRAMES])
        qr_b = place("qr_b", [FRAMES])
        qr_z = place("qr_z", [FRAMES])
        qr_v = place("qr_v", [FRAMES])
        qr = place("qr", [FRAMES])
        kn = place("kn", [TOK])
        pt_f = place("pt_f", [3, P])
        probs = place("probs", [SCORES])
        gate_z = place("gate_z", [FRAMES])
        rk = place("rk", [TOK])
        rv = place("rv", [TOK])
        assert here[0] <= res_at + (KT * FRAMES - 5 * P) * 4
        assert here[0] <= res_at + KT * FRAMES * 4
        here[0] = res_at
        cq_sq = place("cq_sq", [QL // P, FRAMES])
        kv_sq = place("kv_sq", [KVL // P, TOK])
        rx_sd = place("rx_sd", [TOK])
        rstdx2 = place("rstdx2", [TOK])
        cq_var = place("cq_var", [FRAMES])
        cq_f = place("cq_f", [FRAMES])
        kv_var = place("kv_var", [TOK])
        kv_f = place("kv_f", [TOK])
        kr_v = place("kr_v", [TOK])
        v_sb = place("v_sb", [3, P])
        pt_m = place("pt_m", [FRAMES])
        assert here[0] <= res_at + KT * FRAMES * 4
        here[0] = rest_at
        side_lo = place("side_lo", [SIDE_V], F32R)
        ret_s = place("ret_s", [640])
        ret_o = place("ret_o", [FRAMES])
        cen = place("cen", [FRAMES])
        gate = place("gate", [FRAMES])
        stats = place("stats", [8])

        assert here[0] <= nc.sbuf_usable_end

        def bank(name):
            return ctx.enter_context(nc.psum_tensor(name, [P, 512], F32))

        acc = [bank(f"acc{i}") for i in range(2)]
        ps_qn, ps_qr, ps_kn, ps_v, ps_x, ps_y = (bank(n) for n in ("ps_qn", "ps_qr", "ps_kn", "ps_v", "ps_x", "ps_y"))

        ident = consts[:, K_ID:K_ID + P]
        center = consts[:, K_CEN:K_CEN + P]
        ones = consts[:, K_ONE:K_ONE + P]
        dist = consts[:, K_DIST:K_DIST + 640]
        mask = consts[:, K_MASK:K_MASK + SCORES]
        cos_r = consts[:, K_COSR:K_COSR + TOK]
        sin_r = consts[:, K_SINR:K_SINR + TOK]
        eps = consts[:, K_EPS:K_EPS + 1]

        def gain(col):
            return gains[:, bass.ds(col, 1)]

        def halves(t, c, part):
            return t[c % 2][:, part * W // 2:(part + 1) * W // 2]

        def raw_half(c, part):
            return raw[c % RAWS][:, part * W // 2:(part + 1) * W // 2]

        block = ctx.enter_context(nc.Block())

        @block.sync
        def _(sp):
            def load(src, c, more=0):
                if c >= RAWS:
                    sp.wait_ge(sem["lo_ready"], 2 * (c - RAWS) + 2 + 2 * more)
                sp.dma_start(raw[c % RAWS][:], src).then_inc(raw_landed[c % RAWS], 16)

            sp.dma_start(gains[:], gains_in).then_inc(sem["gains_landed"], 16)
            sp.dma_start(x_in[:, 0:4, :], x_all[:, 0:4, :]).then_inc(x_part[0], 16)
            load(w_in[0], 0)
            for n in range(1, 4):
                sp.dma_start(x_in[:, 4 * n:4 * n + 4, :], x_all[:, 4 * n:4 * n + 4, :]).then_inc(x_part[n], 16)
            load(w_in[1], 1)
            sp.dma_start(consts[:], consts_in).then_inc(sem["consts_landed"], 16)
            load(w_in[2], 2)
            load(w_in[3], 3)
            with sp.Fori(0, 8) as i:
                for j in range(4):
                    load(w_in[4 * i + 4 + j], 4 + j, 4 * i)
            for c in range(36, C_WO):
                load(w_in[c], c)
            for j in range(4):
                load(w_o[j], C_WO + j)
            sp.wait_ge(sem["mla_o"], HEADS)
            sp.wait_ge(sem["gate"], HEADS)
            sp.wait_ge(sem["ret_v"], 2 * HEADS)
            sp.dma_start(res[:], x_frames).then_inc(sem["x_back"], 16)
            with sp.Fori(1, KT // 4) as i:
                for j in range(4):
                    load(w_o[4 * i + j], C_WO + j, 4 * i)
            for half in range(2):
                with sp.Fori(0, HALF_F // 4) as i:
                    for j in range(4):
                        load(w_up[4 * i + half * HALF_F + j], C_MLP + half * C_HALF + j, 4 * i)
                with sp.Fori(0, HALF_F // 4) as i:
                    for j in range(4):
                        load(w_down[4 * i + half * HALF_F + j], C_MLP + half * C_HALF + HALF_F + j, 4 * i)
            for q in range(4):
                sp.wait_ge(sem["fin_out"], 4 * q + 4)
                sp.dma_start(out[:, 4 * q:4 * q + 4, :], res[:, 4 * q:4 * q + 4, :]).then_inc(sem["stored"], 16)
            sp.wait_ge(sem["stored"], 64)

        @block.tensor
        def _(pe):
            def mm(o, l, m, start=True, stop=True):
                return pe.matmul(o, l, m, start=start, stop=stop)

            def wide(c, b, wide_of, hi_of, more=0, bmore=0, first=True, last=True, order=None, ready=None):
                a = acc[b % 2]
                order = order or list(range(KT))
                for n, k in enumerate(order):
                    if n % 8 == 0:
                        pe.wait_ge(sem["lo_ready"], 2 * c + n // 8 + 1 + 2 * more)
                    if n == 0 and first and b >= 2:
                        pe.wait_ge(sem["acc_read"], b - 1 + bmore)
                    if ready is not None:
                        ready(k)
                    wh = hi[c % 2][:, k * P:k * P + P]
                    wl = lo[c % 2][:, k * P:k * P + P]
                    end = last and n == KT - 1
                    if end:
                        mm(a[:, FRAMES:], wl, hi_of(k), False, False)
                    m = mm(a[:].rearrange("p (a t) -> p a t", a=2), wh, wide_of(k), first and n == 0, end)
                    if not end:
                        m = mm(a[:, FRAMES:], wl, hi_of(k), False, False)
                    if n % 8 == 7:
                        m.then_inc(sem["chunk_used"], 1)

            def x_wide(k):
                return xs[:, k, :].rearrange("p (a t) -> p a t", a=2)[:, :, META:]

            def x_hi(k):
                return xs[:, k, META:TOK]

            def narrow(c, more=0):
                a = acc[c % 2][:, 0:TOK]
                for k in range(KT):
                    if k % 8 == 0:
                        pe.wait_ge(sem["lo_ready"], 2 * c + k // 8 + 1 + 2 * more)
                    if k == 0:
                        pe.wait_ge(sem["acc_read"], c - 1 + more)
                    wh = hi[c % 2][:, k * P:k * P + P]
                    wl = lo[c % 2][:, k * P:k * P + P]
                    mm(a, wl, xs[:, k, 0:TOK], k == 0, False)
                    mm(a, wh, xs[:, k, TOK:], False, False)
                    m = mm(a, wh, xs[:, k, 0:TOK], False, k == KT - 1)
                    if k % 8 == 7:
                        m.then_inc(sem["chunk_used"], 1)

            def mla_project(h, first=False):
                if first:
                    pe.wait_ge(sem["cq_lo"], 4)
                    pe.wait_ge(sem["kv_lo"], 1)
                else:
                    pe.wait_ge(sem["mla_o"], h)
                pe.wait_ge(sem["side_lo"], h + 1)
                for (o, col, done) in ((ps_qn, SIDE_Q, sem["qn_ps"]), (ps_qr, SIDE_R, sem["qr_ps"])):
                    for k in range(QL // P):
                        wh = side_hi[:, col + k * P:col + (k + 1) * P]
                        wl = side_lo[:, col + k * P:col + (k + 1) * P]
                        end = k == QL // P - 1
                        if end:
                            mm(o[:, FRAMES:], wl, cqs[:, k, 0:FRAMES], False, False)
                        m = mm(o[:], wh, cqs[:, k, :], k == 0, end)
                        if not end:
                            mm(o[:, FRAMES:], wl, cqs[:, k, 0:FRAMES], False, False)
                    m.then_inc(done, 1)
                for k in range(KVL // P):
                    wh = side_hi[:, SIDE_K + k * P:SIDE_K + (k + 1) * P]
                    wl = side_lo[:, SIDE_K + k * P:SIDE_K + (k + 1) * P]
                    mm(ps_kn[:, 0:TOK], wl, ckvs[:, k, 0:TOK], k == 0, False)
                    mm(ps_kn[:, 0:TOK], wh, ckvs[:, k, TOK:], False, False)
                    m = mm(ps_kn[:, 0:TOK], wh, ckvs[:, k, 0:TOK], False, k == KVL // P - 1)
                m.then_inc(sem["kn_ps"], 1)
                for n, (t0, tn) in enumerate(((0, META), (F0, P), (F1, P))):
                    for k in range(KVL // P):
                        m = mm(ps_v[0:tn, n * P:n * P + P], ckv[:, k, t0:t0 + tn],
                               side[:, SIDE_V + k * P:SIDE_V + (k + 1) * P], k == 0, k == KVL // P - 1)
                m.then_inc(sem["v_ps"], 1)

            def mla_scores(h):
                pe.wait_ge(sem["qn_ready"], h + 1)
                pe.wait_ge(sem["kn_ready"], h + 1)
                pe.wait_ge(sem["qr_ready"], h + 1)
                for n, (c0, keys) in enumerate(((0, Q0K), (Q0K, Q1K))):
                    mm(ps_qn[:, c0:c0 + keys], qn[:, n * P:n * P + P], kn[:, 0:keys], True, False)
                    m = mm(ps_qn[:, c0:c0 + keys], qr[0:ROPE, n * P:n * P + P], kr[0:ROPE, 0:keys], False, True)
                m.then_inc(sem["mla_s_ps"], 1)

            def mla_turn(h):
                pe.wait_ge(sem["mla_p"], 2 * h + 2)
                pe.wait_ge(sem["v_ready"], 2 * h + 2)
                for n, c0 in enumerate((0, Q0K)):
                    pe.transpose(ps_v[0:META, n * P:n * P + P], probs[:, c0:c0 + META], ident)
                    pe.transpose(ps_kn[:, n * P:n * P + P], probs[:, c0 + F0:c0 + F0 + P], ident)
                pe.transpose(ps_kn[:, 2 * P:3 * P], probs[:, Q0K + F1:Q0K + F1 + P], ident).then_inc(sem["pt_ps"], 1)

            def mla_values(h):
                pe.wait_ge(sem["pt_f"], h + 1)
                pe.wait_ge(sem["pt_m"], h + 1)
                mm(ps_qn[:, 0:FRAMES], v_sb[:, 1, :], pt_f[:, 0:2, :].rearrange("p a t -> p (a t)"), True, False)
                mm(ps_qn[:, P:FRAMES], v_sb[:, 2, :], pt_f[:, 2, :], False, False)
                mm(ps_qn[:, 0:FRAMES], v_sb[:, 0, :], pt_m[:], False, True).then_inc(sem["mla_o_ps"], 1)

            def ret_scores(g, first=False):
                pe.wait_ge(sem["rq_ready"], g + 1)
                pe.wait_ge(sem["rk_ready"], g + 1)
                pe.wait_ge(sem["acc_read"], C_HEAD + 4 * g)
                if not first:
                    pe.wait_ge(sem["ret_sd"], g)
                mm(ps_x[:, 0:FRAMES], rk[:, F0:F0 + P], rq[:])
                mm(ps_x[0:META, FRAMES:], rk[:, 0:META], rq[:]).then_inc(sem["ret_s_ps"], 1)
                mm(ps_y[:, 0:P], rk[:, F1:F1 + P], rq[:, P:])
                pe.transpose(ps_y[0:META, P:2 * P], rv[:, 0:META], ident)
                pe.transpose(ps_y[:, 2 * P:3 * P], rv[:, F0:F0 + P], ident)
                pe.transpose(ps_y[:, 3 * P:4 * P], rv[:, F1:F1 + P], ident).then_inc(sem["ret_y_ps"], 1)

            def ret_values(g):
                pe.wait_ge(sem["ret_s"], 3 * g + 3)
                pe.wait_ge(sem["ret_v"], 2 * g + 2)
                mm(ps_qr[:, 0:FRAMES], ret_v[:, 1, :], ret_s[:, 0:FRAMES], True, False)
                mm(ps_qr[:, P:FRAMES], ret_v[:, 2, :], ret_s[:, FRAMES:FRAMES + P], False, False)
                mm(ps_qr[:, 0:FRAMES], ret_v[:, 0, :], ret_s[:, FRAMES + P:], False, True).then_inc(sem["ret_o_ps"], 1)

            def ret_center(g):
                pe.wait_ge(sem["ret_o"], g + 1)
                mm(ps_x[:, 0:FRAMES], center, ret_o[:]).then_inc(sem["cen_ps"], 1)

            def ret_var(g):
                pe.wait_ge(sem["ret_sq"], g + 1)
                mm(ps_y[:, 0:FRAMES], ones, sq[:]).then_inc(sem["var_ps"], 1)

            def x_parts(k):
                pe.wait_ge(sem["x_lo"], k + 1)

            wide(0, 0, x_wide, x_hi, ready=x_parts)
            for c in range(1, 4):
                wide(c, c, x_wide, x_hi)
            narrow(4)
            pe.wait_ge(sem["consts_landed"], 16)
            pe.wait_ge(sem["ssx"], 5)
            mm(ps_x[:, 0:TOK], ones, x_sq[:, 0, :]).then_inc(sem["ss_x_ps"], 1)
            pe.wait_ge(sem["cq_sum"], 2)
            mm(ps_y[:, 0:FRAMES], ones, cq_sq[:, 0, :]).then_inc(sem["ss_q_ps"], 1)
            narrow(5)
            narrow(6)
            pe.wait_ge(sem["kv_sum"], 1)
            mm(ps_v[:, 0:TOK], ones, kv_sq[:, 0, :]).then_inc(sem["ss_k_ps"], 1)

            wide(C_HEAD0, C_HEAD0, x_wide, x_hi)
            mla_project(0, True)
            narrow(C_HEAD0 + 1)
            mla_scores(0)
            narrow(C_HEAD0 + 2)
            mla_turn(0)
            mla_values(0)

            def head(h, i, first=False):
                c = C_HEAD
                m = 4 * i
                wide(c, c, x_wide, x_hi, m, m)
                mla_project(h)
                ret_scores(h - 1, first)
                wide(c + 1, c + 1, x_wide, x_hi, m, m)
                mla_scores(h)
                ret_values(h - 1)
                narrow(c + 2, m)
                mla_turn(h)
                ret_center(h - 1)
                narrow(c + 3, m)
                mla_values(h)
                ret_var(h - 1)

            head(1, 0, True)
            with pe.Fori(1, HEADS - 1) as i:
                head(i + 1, i)

            wide(C_GATE7, C_GATE7, x_wide, x_hi)
            pe.wait_ge(sem["mla_ss"], HEADS)
            mm(ps_kn[:, 0:FRAMES], ones, sum_sq[:]).then_inc(sem["mla_ss_ps"], 1)
            ret_scores(HEADS - 1)
            ret_values(HEADS - 1)
            ret_center(HEADS - 1)
            ret_var(HEADS - 1)

            def hid_wide(k):
                return hid[:, k, :].rearrange("p (a t) -> p a t", a=2)

            def hid_hi(k):
                return hid[:, k, 0:FRAMES]

            def wo_block(c, more=0):
                wide(c, c, hid_wide, hid_hi, more, more)

            def mixed(k):
                if k < HEADS:
                    pe.wait_ge(sem["ret_lo"], k + 1)
                else:
                    pe.wait_ge(sem["mla_lo"], k - HEADS + 1)

            wide(C_WO, C_WO, hid_wide, hid_hi, ready=mixed)
            for j in range(1, 4):
                wo_block(C_WO + j)
            with pe.Fori(1, KT // 4) as i:
                for j in range(4):
                    wo_block(C_WO + j, 4 * i)

            for half in range(2):
                c0, b0 = C_MLP + half * C_HALF, C_MLP + half * B_HALF

                def m_parts(k):
                    pe.wait_ge(sem["m_lo"], k + 1)

                def up(j, more=0, ready=None):
                    wide(c0 + j, b0 + j, x_wide, x_hi, more, more, ready=ready)

                up(0, ready=m_parts if half == 0 else None)
                if half == 0:
                    pe.wait_ge(sem["h_ss"], KT)
                    mm(ps_x[:, 0:FRAMES], ones, sum_sq[:]).then_inc(sem["h_ss_ps"], 1)
                for j in range(1, 4):
                    up(j)
                with pe.Fori(1, HALF_F // 4) as i:
                    for j in range(4):
                        up(j, 4 * i)

                cd, bd = c0 + HALF_F, b0 + HALF_F

                def down(n, more=0, bmore=0, guard=False):
                    for part in range(DOWN_PER_BLOCK):
                        def up_parts(k, part=part):
                            pe.wait_ge(sem["up_lo"], half * HALF_F + part * KT + k + 1)
                        wide(cd + DOWN_PER_BLOCK * n + part, bd + n, lambda k: hid_wide(part * KT + k),
                             lambda k: hid_hi(part * KT + k), more, bmore, first=part == 0,
                             last=part == DOWN_PER_BLOCK - 1, ready=up_parts if guard else None)

                down(0, guard=True)
                down(1)
                with pe.Fori(1, KT // 2) as i:
                    down(0, 4 * i, 2 * i)
                    down(1, 4 * i, 2 * i)

            pe.wait_ge(sem["dn_ss"], 2 * KT)
            mm(ps_x[:, 0:FRAMES], ones, sum_sq[:]).then_inc(sem["fin_ps"], 1)

        @block.scalar
        def _(act):
            def copy(o, i):
                return act.activation(o, i, ACT.Copy)

            def split_hi(c, part, more=0):
                if c < 0 or c >= C_END:
                    return
                if part == 0:
                    act.wait_ge(raw_landed[c % RAWS], 16 * (c // RAWS + 1) + 4 * more)
                if c >= 2:
                    act.wait_ge(sem["chunk_used"], 2 * (c - 2) + part + 1 + 2 * more)
                copy(halves(hi, c, part), raw_half(c, part)).then_inc(sem["hi_ready"], 1)

            def b_copy(c, w, more=0):
                act.wait_ge(sem["chunk_used"], 2 * c + 2 + 2 * more)
                return copy(half_b[w % 2][:], acc_of[0][:, FRAMES:]).then_inc(sem["half_b"], 1)

            acc_of = [None]

            def wide_block(c, b, w, more=0, ahead=True):
                acc_of[0] = acc[b % 2]
                if ahead:
                    split_hi(c + 2, 0, more)
                b_copy(c, w, more)
                if ahead:
                    split_hi(c + 2, 1, more)

            def side_load(h):
                act.dma_start(side[:], w_side[h]).then_inc(sem["side_landed"], 16)

            def side_split(h):
                act.wait_ge(sem["side_landed"], 16 * h + 16)
                copy(side_hi[:], side[:, 0:SIDE_V]).then_inc(sem["side_hi"], 1)

            act.wait_ge(sem["gains_landed"], 16)

            def x_round(k):
                act.wait_ge(x_part[k // 4], 16)
                act.activation(xs[:, k, 0:TOK], x_in[:, k, :], ACT.Identity, scale=gain(G_MIX + k)).then_inc(sem["x_hi"], 1)

            for k in range(3):
                x_round(k)
            split_hi(0, 0)
            for k in range(3, 8):
                x_round(k)
            split_hi(0, 1)
            for k in range(8, 16):
                x_round(k)
            split_hi(1, 0)
            split_hi(1, 1)

            for c in range(4):
                wide_block(c, c, c)
            act.wait_ge(sem["acc_read"], 4)
            act.activation(cq_sq[:], cq[:], ACT.Square).then_inc(sem["cq_sq"], 1)
            split_hi(6, 0)
            split_hi(6, 1)
            act.wait_ge(sem["ss_x_ps"], 1)
            act.activation(rx_sd[:], ps_x[:, 0:TOK], ACT.Sqrt, bias=eps, scale=1.0 / D).then_inc(sem["rx_sd"], 1)
            act.wait_ge(sem["x_lo"], KT)
            side_load(0)
            act.wait_ge(sem["rq_var"], 1)
            act.activation(cq_f[:], cq_var[:], ACT.Sqrt, bias=eps, scale=1.0 / QL).then_inc(sem["cq_sd"], 1)
            split_hi(7, 0)
            act.wait_ge(sem["acc_read"], C_KR)
            act.activation(kv_sq[:], ckv[:], ACT.Square).then_inc(sem["kv_sq"], 1)
            split_hi(7, 1)
            for k in range(QL // P):
                act.wait_ge(sem["cq_scaled"], k + 1)
                copy(cqs[:, k, 0:FRAMES], cq[:, k, :]).then_inc(sem["cq_hi"], 1)
            split_hi(8, 0)
            act.wait_ge(sem["chunk_used"], 2 * C_KR + 2)
            copy(zk[:], acc[C_KR % 2][:, 0:TOK]).then_inc(sem["acc_read"], 1)
            split_hi(8, 1)
            act.wait_ge(sem["rq_var"], 2)
            act.activation(kv_f[:], kv_var[:], ACT.Sqrt, bias=eps, scale=1.0 / KVL).then_inc(sem["kv_sd"], 1)
            act.wait_ge(sem["kv_scaled"], 2)
            copy(ckvs[:, :, 0:TOK], ckv[:]).then_inc(sem["kv_hi"], 1)
            side_split(0)

            def q_block(h, c, w, more):
                wide_block(c, c, w, more)
                act.wait_ge(sem["acc_read"], c + 1 + more)
                copy(swq[0:64, :], zq[64:128, :]).then_inc(sem["rq_sw"], 1)
                copy(swq[64:128, :], zq[0:64, :]).then_inc(sem["rq_sw"], 1)

            def k_block(h, c, more):
                split_hi(c + 2, 0, more)
                act.wait_ge(sem["chunk_used"], 2 * c + 2 + 2 * more)
                a = acc[c % 2]
                copy(zk[:], a[:, 0:TOK])
                copy(swk[0:64, :], a[64:128, 0:TOK])
                copy(swk[64:128, :], a[0:64, 0:TOK]).then_inc(sem["acc_read"], 1)
                split_hi(c + 2, 1, more)

            def v_block(h, c, more):
                split_hi(c + 2, 0, more)
                split_hi(c + 2, 1, more)

            def mla_in(h):
                act.wait_ge(sem["qn_ps"], h + 1)
                copy(qn_b[:], ps_qn[:, FRAMES:]).then_inc(sem["qn_b"], 1)
                act.wait_ge(sem["qr_ps"], h + 1)
                copy(qr_b[:], ps_qr[:, FRAMES:]).then_inc(sem["qr_b"], 1)
                act.wait_ge(sem["v_ps"], h + 1)
                copy(v_sb[0:META, 0, :], ps_v[0:META, 0:P]).then_inc(sem["v_ready"], 1)
                copy(v_sb[:, 1:3, :].rearrange("p a t -> p (a t)"), ps_v[:, P:3 * P]).then_inc(sem["v_ready"], 1)

            def mla_exp(h):
                for n, (c0, keys) in enumerate(((0, Q0K), (Q0K, Q1K))):
                    act.wait_ge(sem["mla_max"], 2 * h + n + 1)
                    act.activation(probs[:, c0:c0 + keys], probs[:, c0:c0 + keys], ACT.Exp, bias=stats[:, n:n + 1],
                                   accum_out=stats[:, 2 + n:3 + n]).then_inc(sem["mla_exp"], 1)

            def mla_turned(h):
                act.wait_ge(sem["pt_ps"], h + 1)
                copy(pt_m[0:META, :], ps_v[0:META, 0:FRAMES]).then_inc(sem["pt_m"], 1)

            def mla_square(h):
                act.wait_ge(sem["mla_o"], h + 1)
                act.activation(t2[:], mla_o[:, h, :], ACT.Square).then_inc(sem["mla_sq"], 1)

            def ret_decay(g, first=False):
                if not first:
                    act.wait_ge(sem["ret_s"], 3 * g)
                act.activation(decay[:], dist, ACT.Exp, scale=consts[:, bass.ds(K_LG + g, 1)]).then_inc(sem["decay"], 1)

            def ret_out(g):
                act.wait_ge(sem["ret_o_ps"], g + 1)
                copy(ret_o[:], ps_qr[:, 0:FRAMES]).then_inc(sem["ret_o"], 1)

            def ret_square(g):
                act.wait_ge(sem["cen"], g + 1)
                act.activation(sq[:], cen[:], ACT.Square).then_inc(sem["ret_sq"], 1)

            def ret_root(g):
                act.wait_ge(sem["var_ps"], g + 1)
                act.activation(z[:], ps_y[:, 0:FRAMES], ACT.Sqrt, bias=eps, scale=1.0 / HD).then_inc(sem["ret_sd"], 1)

            def ret_round(g):
                act.wait_ge(sem["ret_a"], g + 1)
                copy(hid[:, g, 0:FRAMES], ret_o[:]).then_inc(sem["ret_hi"], 1)

            def gate_exp(g):
                act.wait_ge(sem["gate_z"], g + 1)
                act.activation(gate[:], gate_z[:], ACT.Exp, scale=-1.0).then_inc(sem["gate_exp"], 1)

            q_block(0, C_HEAD0, W_HEAD0, 0)
            mla_in(0)
            k_block(0, C_HEAD0 + 1, 0)
            mla_exp(0)
            act.wait_ge(sem["v_ps"], 1)
            side_load(1)
            v_block(0, C_HEAD0 + 2, 0)
            mla_turned(0)
            mla_square(0)
            side_split(1)

            def head(h, i, first=False, last=False):
                c, m = C_HEAD, 4 * i
                wide_block(c, c, W_HEAD, m)
                ret_decay(h - 1, first)
                mla_in(h)
                gate_exp(h - 1)
                q_block(h, c + 1, W_HEAD + 1, m)
                ret_out(h - 1)
                mla_exp(h)
                if not last:
                    act.wait_ge(sem["v_ps"], h + 1)
                    side_load(h + 1)
                k_block(h, c + 2, m)
                mla_turned(h)
                ret_square(h - 1)
                v_block(h, c + 3, m)
                mla_square(h)
                ret_root(h - 1)
                ret_round(h - 1)
                if not last:
                    side_split(h + 1)

            head(1, 0, True)
            with act.Fori(1, HEADS - 2) as i:
                head(i + 1, i)
            head(HEADS - 1, HEADS - 2, last=True)

            g = HEADS - 1
            wide_block(C_GATE7, C_GATE7, W_GATE7)
            ret_decay(g)
            act.wait_ge(sem["mla_ss_ps"], 1)
            act.activation(rstd[:], ps_kn[:, 0:FRAMES], ACT.Sqrt, bias=eps, scale=1.0 / (HEADS * HD)).then_inc(sem["mla_sd"], 1)
            gate_exp(g)
            ret_out(g)
            ret_square(g)
            for k in range(HEADS):
                act.wait_ge(sem["mla_a"], k + 1)
                copy(hid[:, HEADS + k, 0:FRAMES], mla_o[:, k, :]).then_inc(sem["mla_hi"], 1)
                if k == 1:
                    ret_root(g)
            ret_round(g)

            def wo_block(j, j0, more=0):
                wide_block(C_WO + j0, C_WO + j0, W_WO + j0, more)
                act.wait_ge(sem["acc_read"], C_WO + j0 + 1 + more)
                act.activation(sq[:], res[:, j, :], ACT.Square).then_inc(sem["h_sq"], 1)
                act.activation(xs[:, j, META:TOK], res[:, j, :], ACT.Identity,
                               scale=gain(G_MLP + j)).then_inc(sem["m_hi"], 1)

            with act.Fori(0, KT // 4) as i:
                for j in range(4):
                    wo_block(4 * i + j, j, 4 * i)

            for half in range(2):
                c0, b0, w0 = C_MLP + half * C_HALF, C_MLP + half * B_HALF, W_MLP + half * B_HALF

                def up(n, j0, more=0, root=False):
                    wide_block(c0 + j0, b0 + j0, w0 + j0, more)
                    if root:
                        act.wait_ge(sem["h_ss_ps"], 1)
                        act.activation(rstd[:], ps_x[:, 0:FRAMES], ACT.Sqrt, bias=eps, scale=1.0 / D).then_inc(sem["h_sd"], 1)
                    act.wait_ge(sem["up_r"], n + 1 + half * HALF_F)
                    act.activation(sq[:], r[:], ACT.Square).then_inc(sem["up_sq"], 1)
                    act.activation(hid[:, n, 0:FRAMES], r[:], ACT.Square).then_inc(sem["up_hi"], 1)

                if half == 1:
                    act.wait_ge(sem["dn_ss"], KT)
                for j in range(4):
                    up(j, j, root=half == 0 and j == 0)
                with act.Fori(1, HALF_F // 4) as i:
                    for j in range(4):
                        up(4 * i + j, j, 4 * i)

                cd, bd, wd = c0 + HALF_F, b0 + HALF_F, w0 + HALF_F

                def down(n, j0, more=0, ahead=True):
                    c = cd + 2 * j0
                    if ahead:
                        split_hi(c + 2, 0, more)
                        split_hi(c + 2, 1, more)
                    wide_block(c + 1, bd + j0, wd + j0, more, ahead)
                    act.wait_ge(sem["acc_read"], bd + n + 1)
                    act.activation(sq[:], res[:, n, :], ACT.Square).then_inc(sem["dn_sq"], 1)

                with act.Fori(0, KT // 2 - 1) as i:
                    for j in range(2):
                        down(2 * i + j, j, 4 * i)
                down(KT - 2, 0, 4 * (KT // 2 - 1), True)
                down(KT - 1, 1, 4 * (KT // 2 - 1), half == 0)

            act.wait_ge(sem["fin_ps"], 1)
            act.activation(z[:], ps_x[:, 0:FRAMES], ACT.Sqrt, bias=eps, scale=1.0 / D).then_inc(sem["fin_sd"], 1)

        @block.vector
        def _(dve):
            def tt(o, a, b, op):
                return dve.tensor_tensor(o, a, b, op)

            def split_lo(c, part, more=0):
                if c >= C_END:
                    return
                dve.wait_ge(sem["hi_ready"], 2 * c + part + 1 + 2 * more)
                tt(halves(lo, c, part), raw_half(c, part), halves(hi, c, part).bitcast(F32),
                   ALU.subtract).then_inc(sem["lo_ready"], 1)

            def sum_ab(o, b, w, wmore=0):
                dve.wait_ge(sem["half_b"], w + 1 + wmore)
                return tt(o, acc[b % 2][:, 0:FRAMES], half_b[w % 2][:], ALU.add)

            def x_rest(k):
                dve.wait_ge(sem["x_hi"], k + 1)
                dve.scalar_tensor_tensor(out=xs[:, k, TOK:], in0=x_in[:, k, :], scalar=gain(G_MIX + k),
                                         in1=xs[:, k, 0:TOK].bitcast(F32), op0=ALU.mult,
                                         op1=ALU.subtract).then_inc(sem["x_lo"], 1)

            dve.wait_ge(sem["gains_landed"], 16)
            for k in range(3):
                dve.wait_ge(x_part[0], 16)
                x_rest(k)
            split_lo(0, 0)
            for k in range(3, 8):
                x_rest(k)
            split_lo(0, 1)
            for k in range(8, 16):
                x_rest(k)
            split_lo(1, 0)
            split_lo(1, 1)
            for c in range(4):
                split_lo(c + 2, 0)
                sum_ab(cq[:, c, :], c, c).then_inc(sem["acc_read"], 1)
                split_lo(c + 2, 1)
            dve.wait_ge(sem["consts_landed"], 16)
            dve.wait_ge(sem["cq_sq"], 1)
            tt(cq_sq[:, 0:2, :], cq_sq[:, 0:2, :], cq_sq[:, 2:4, :], ALU.add).then_inc(sem["cq_sum"], 1)
            dve.wait_ge(sem["cq_sum"], 1)
            tt(cq_sq[:, 0, :], cq_sq[:, 0, :], cq_sq[:, 1, :], ALU.add).then_inc(sem["cq_sum"], 1)
            split_lo(6, 0)
            split_lo(6, 1)
            dve.wait_ge(sem["chunk_used"], 2 * C_KV + 2)
            dve.tensor_copy(ckv[:, 0, :], acc[C_KV % 2][:, 0:TOK]).then_inc(sem["acc_read"], 1)
            dve.wait_ge(sem["rx_sd"], 1)
            dve.reciprocal(rstdx[:], rx_sd[:]).then_inc(sem["rstdx"], 1)
            dve.wait_ge(sem["rstdx"], 1)
            tt(rstdx2[:], rstdx[:], rstdx[:], ALU.mult).then_inc(sem["stat"], 1)
            dve.wait_ge(sem["stat"], 1)
            dve.wait_ge(sem["ss_q_ps"], 1)
            tt(cq_var[:], ps_y[:, 0:FRAMES], rstdx2[:, META:], ALU.mult).then_inc(sem["rq_var"], 1)
            dve.wait_ge(sem["cq_sd"], 1)
            dve.reciprocal(cq_var[:], cq_f[:]).then_inc(sem["stat"], 1)
            dve.wait_ge(sem["stat"], 2)
            tt(cq_f[:], cq_var[:], rstdx[:, META:], ALU.mult).then_inc(sem["stat"], 1)
            dve.wait_ge(sem["stat"], 3)
            for k in range(QL // P):
                dve.scalar_tensor_tensor(out=cq[:, k, :], in0=cq[:, k, :], scalar=gain(G_Q + k), in1=cq_f[:],
                                         op0=ALU.mult, op1=ALU.mult).then_inc(sem["cq_scaled"], 1)
            split_lo(7, 0)
            dve.wait_ge(sem["chunk_used"], 2 * C_KV + 4)
            dve.tensor_copy(ckv[:, 1, :], acc[(C_KV + 1) % 2][:, 0:TOK]).then_inc(sem["acc_read"], 1)
            dve.wait_ge(sem["kv_sq"], 1)
            tt(kv_sq[:, 0, :], kv_sq[:, 0, :], kv_sq[:, 1, :], ALU.add).then_inc(sem["kv_sum"], 1)
            split_lo(7, 1)
            for k in range(QL // P):
                dve.wait_ge(sem["cq_hi"], k + 1)
                tt(cqs[:, k, FRAMES:], cq[:, k, :], cqs[:, k, 0:FRAMES].bitcast(F32), ALU.subtract).then_inc(sem["cq_lo"], 1)
            split_lo(8, 0)
            tt(cos_r, cos_r, rstdx[:], ALU.mult).then_inc(sem["tables"], 1)
            tt(sin_r, sin_r, rstdx[:], ALU.mult).then_inc(sem["tables"], 1)
            dve.wait_ge(sem["acc_read"], C_KR + 1)
            tt(kr[0:ROPE, :], zk[0:ROPE, :], consts[0:ROPE, K_COSM:K_COSM + TOK], ALU.mult).then_inc(sem["kr_raw"], 1)
            tt(kr_v[0:ROPE, :], zk[ROPE:, :], consts[ROPE:, K_SINM:K_SINM + TOK], ALU.mult).then_inc(sem["kr_raw"], 1)
            dve.wait_ge(sem["kr_raw"], 2)
            tt(kr[0:ROPE, :], kr[0:ROPE, :], kr_v[0:ROPE, :], ALU.add).then_inc(sem["kr_raw"], 1)
            dve.wait_ge(sem["kr_raw"], 3)
            tt(kr[0:ROPE, :], kr[0:ROPE, :], rstdx[0:ROPE, :], ALU.mult).then_inc(sem["kr_ready"], 1)
            split_lo(8, 1)
            dve.wait_ge(sem["ss_k_ps"], 1)
            tt(kv_var[:], ps_v[:, 0:TOK], rstdx2[:], ALU.mult).then_inc(sem["rq_var"], 1)
            dve.wait_ge(sem["kv_sd"], 1)
            dve.reciprocal(kv_var[:], kv_f[:]).then_inc(sem["stat"], 1)
            dve.wait_ge(sem["stat"], 4)
            tt(kv_f[:], kv_var[:], rstdx[:], ALU.mult).then_inc(sem["stat"], 1)
            dve.wait_ge(sem["stat"], 5)
            for k in range(KVL // P):
                dve.scalar_tensor_tensor(out=ckv[:, k, :], in0=ckv[:, k, :], scalar=gain(G_KV + k), in1=kv_f[:],
                                         op0=ALU.mult, op1=ALU.mult).then_inc(sem["kv_scaled"], 1)
            dve.wait_ge(sem["kv_hi"], 1)
            tt(ckvs[:, :, TOK:], ckv[:], ckvs[:, :, 0:TOK].bitcast(F32), ALU.subtract).then_inc(sem["kv_lo"], 1)

            def side_rest(h):
                dve.wait_ge(sem["side_hi"], h + 1)
                tt(side_lo[:], side[:, 0:SIDE_V], side_hi[:].bitcast(F32), ALU.subtract).then_inc(sem["side_lo"], 1)

            def q_sum(h, c, w, m, wm):
                split_lo(c + 2, 0, m)
                sum_ab(zq[:], c, w, wm).then_inc(sem["acc_read"], 1)
                split_lo(c + 2, 1, m)

            def q_rope(h):
                dve.wait_ge(sem["rq_sw"], 2 * h + 2)
                tt(swq[:], swq[:], sin_r[:, META:], ALU.mult).then_inc(sem["rq_sin"], 1)
                dve.wait_ge(sem["rq_sin"], h + 1)
                dve.wait_ge(sem["rq_cos"], h + 1)
                tt(rq[:], rq[:], swq[:], ALU.add).then_inc(sem["rq_ready"], 1)

            def k_rope(h, c, m):
                split_lo(c + 2, 0, m)
                dve.wait_ge(sem["acc_read"], c + 1 + m)
                tt(swk[:], swk[:], sin_r, ALU.mult).then_inc(sem["rk_sin"], 1)
                split_lo(c + 2, 1, m)
                dve.wait_ge(sem["rk_sin"], h + 1)
                dve.wait_ge(sem["rk_cos"], h + 1)
                tt(rk[:], rk[:], swk[:], ALU.add).then_inc(sem["rk_ready"], 1)

            def v_norm(h, c, m):
                split_lo(c + 2, 0, m)
                dve.wait_ge(sem["chunk_used"], 2 * c + 2 + 2 * m)
                tt(rv[:], acc[c % 2][:, 0:TOK], rstdx[:], ALU.mult).then_inc(sem["acc_read"], 1)
                split_lo(c + 2, 1, m)

            def mla_in(h):
                dve.wait_ge(sem["qn_b"], h + 1)
                tt(qn[:], ps_qn[:, 0:FRAMES], qn_b[:], ALU.add).then_inc(sem["qn_ready"], 1)
                dve.wait_ge(sem["qr_b"], h + 1)
                tt(qr_z[:], ps_qr[:, 0:FRAMES], qr_b[:], ALU.add).then_inc(sem["qr_raw"], 1)
                dve.wait_ge(sem["kn_ps"], h + 1)
                dve.tensor_copy(kn[:], ps_kn[:, 0:TOK]).then_inc(sem["kn_ready"], 1)
                dve.wait_ge(sem["qr_raw"], h + 1)
                tt(qr_v[0:ROPE, :], qr_z[ROPE:, :], consts[ROPE:, K_SINM + META:K_SINM + TOK], ALU.mult).then_inc(sem["qr_u"], 1)
                dve.wait_ge(sem["qr_u"], 2 * h + 2)
                tt(qr[0:ROPE, :], qr[0:ROPE, :], qr_v[0:ROPE, :], ALU.add).then_inc(sem["qr_ready"], 1)

            def mla_softmax(h):
                dve.wait_ge(sem["mla_s_ps"], h + 1)
                dve.scalar_tensor_tensor(out=probs[:], in0=ps_qn[:, 0:SCORES], scalar=float((NOPE + ROPE) ** -0.5),
                                         in1=mask, op0=ALU.mult, op1=ALU.add).then_inc(sem["mla_s"], 1)
                dve.wait_ge(sem["mla_s"], h + 1)
                for n, (c0, keys) in enumerate(((0, Q0K), (Q0K, Q1K))):
                    dve.tensor_reduce(stats[:, n:n + 1], probs[:, c0:c0 + keys], AX.X, ALU.max,
                                      negate=True).then_inc(sem["mla_max"], 1)

            def mla_norm(h):
                dve.wait_ge(sem["mla_exp"], 2 * h + 2)
                dve.reciprocal(stats[:, 4:6], stats[:, 2:4]).then_inc(sem["mla_inv"], 1)
                dve.wait_ge(sem["mla_inv"], h + 1)
                for n, (c0, keys) in enumerate(((0, Q0K), (Q0K, Q1K))):
                    dve.tensor_scalar(probs[:, c0:c0 + keys], probs[:, c0:c0 + keys], stats[:, 4 + n:5 + n], None,
                                      ALU.mult).then_inc(sem["mla_p"], 1)

            def mla_turned(h):
                dve.wait_ge(sem["pt_ps"], h + 1)
                dve.tensor_copy(pt_f[:].rearrange("p a t -> p (a t)"), ps_kn[:, 0:3 * P]).then_inc(sem["pt_f"], 1)

            def mla_out(h):
                dve.wait_ge(sem["mla_o_ps"], h + 1)
                dve.tensor_copy(mla_o[:, h, :], ps_qn[:, 0:FRAMES]).then_inc(sem["mla_o"], 1)

            def ret_in(g):
                dve.wait_ge(sem["decay"], g + 1)
                dve.wait_ge(sem["ret_s_ps"], g + 1)
                scale = float(HD ** -0.5)

                def decayed(o, i, d):
                    dve.scalar_tensor_tensor(out=o, in0=i, scalar=scale, in1=d, op0=ALU.mult,
                                             op1=ALU.mult).then_inc(sem["ret_s"], 1)

                decayed(ret_s[:, 0:FRAMES], ps_x[:, 0:FRAMES], decay[:, 0:FRAMES])
                decayed(ret_s[0:META, FRAMES + P:], ps_x[0:META, FRAMES:], decay[0:META, FRAMES + P:])
                dve.wait_ge(sem["ret_y_ps"], g + 1)
                decayed(ret_s[:, FRAMES:FRAMES + P], ps_y[:, 0:P], decay[:, FRAMES:FRAMES + P])
                dve.tensor_copy(ret_v[0:META, 0, :], ps_y[0:META, P:2 * P]).then_inc(sem["ret_v"], 1)
                dve.tensor_copy(ret_v[:, 1:3, :].rearrange("p a t -> p (a t)"), ps_y[:, 2 * P:]).then_inc(sem["ret_v"], 1)

            def ret_centered(g):
                dve.wait_ge(sem["cen_ps"], g + 1)
                dve.tensor_copy(cen[:], ps_x[:, 0:FRAMES]).then_inc(sem["cen"], 1)

            def ret_norm(g):
                dve.wait_ge(sem["ret_sd"], g + 1)
                dve.reciprocal(r[:], z[:]).then_inc(sem["ret_inv"], 1)
                dve.wait_ge(sem["ret_inv"], g + 1)
                tt(r[:], cen[:], r[:], ALU.mult).then_inc(sem["ret_y"], 1)
                dve.wait_ge(sem["ret_y"], g + 1)
                dve.wait_ge(sem["gate"], g + 1)
                dve.scalar_tensor_tensor(out=ret_o[:], in0=r[:], scalar=gain(G_RET + g), in1=gate[:], op0=ALU.mult,
                                         op1=ALU.mult).then_inc(sem["ret_a"], 1)

            def ret_rest(g):
                dve.wait_ge(sem["ret_hi"], g + 1)
                tt(hid[:, g, FRAMES:], ret_o[:], hid[:, g, 0:FRAMES].bitcast(F32), ALU.subtract).then_inc(sem["ret_lo"], 1)

            def gate_sum(g, c, w, m, wm):
                split_lo(c + 2, 0, m)
                sum_ab(gate_z[:], c, w, wm).then_inc(sem["acc_read"], 1)
                split_lo(c + 2, 1, m)

            def gate_inv(g):
                dve.wait_ge(sem["gate_exp"], g + 1)
                dve.tensor_scalar(gate[:], gate[:], 1.0, None, ALU.add).then_inc(sem["gate_den"], 1)
                dve.wait_ge(sem["gate_den"], g + 1)
                dve.reciprocal(gate[:], gate[:]).then_inc(sem["gate_inv"], 1)

            side_rest(0)
            q_sum(0, C_HEAD0, W_HEAD0, 0, 0)
            mla_in(0)
            q_rope(0)
            k_rope(0, C_HEAD0 + 1, 0)
            mla_softmax(0)
            mla_norm(0)
            v_norm(0, C_HEAD0 + 2, 0)
            mla_turned(0)
            mla_out(0)
            side_rest(1)

            def head(h, i, last=False):
                c, m = C_HEAD, 4 * i
                gate_sum(h - 1, c, W_HEAD, m, 2 * i)
                mla_in(h)
                ret_in(h - 1)
                gate_inv(h - 1)
                q_sum(h, c + 1, W_HEAD + 1, m, 2 * i)
                mla_softmax(h)
                q_rope(h)
                mla_norm(h)
                k_rope(h, c + 2, m)
                mla_turned(h)
                ret_centered(h - 1)
                v_norm(h, c + 3, m)
                mla_out(h)
                ret_norm(h - 1)
                ret_rest(h - 1)
                if not last:
                    side_rest(h + 1)

            with dve.Fori(0, HEADS - 2) as i:
                head(i + 1, i)
            head(HEADS - 1, HEADS - 2, last=True)

            g = HEADS - 1
            gate_sum(g, C_GATE7, W_GATE7, 0, 0)
            ret_in(g)
            dve.wait_ge(sem["mla_sd"], 1)
            dve.reciprocal(rstd[:], rstd[:]).then_inc(sem["mla_rstd"], 1)
            dve.wait_ge(sem["mla_rstd"], 1)

            def mla_scale(k):
                dve.scalar_tensor_tensor(out=mla_o[:, k, :], in0=mla_o[:, k, :], scalar=gain(G_MLA + k), in1=rstd[:],
                                         op0=ALU.mult, op1=ALU.mult).then_inc(sem["mla_a"], 1)

            def mla_rest(k):
                dve.wait_ge(sem["mla_hi"], k + 1)
                tt(hid[:, HEADS + k, FRAMES:], mla_o[:, k, :], hid[:, HEADS + k, 0:FRAMES].bitcast(F32),
                   ALU.subtract).then_inc(sem["mla_lo"], 1)

            gate_inv(g)
            ret_centered(g)
            for k in range(4):
                mla_scale(k)
            for k in range(2):
                mla_rest(k)
            ret_norm(g)
            for k in range(4, HEADS):
                mla_scale(k)
            for k in range(2, HEADS):
                mla_rest(k)
            ret_rest(g)

            def residual(n, b, res_ready):
                dve.wait_ge(res_ready[0], res_ready[1])
                tt(res[:, n, :], acc[b % 2][:, 0:FRAMES], t2[:], ALU.add).then_inc(sem["acc_read"], 1)

            def wo_block(j, j0, m=0):
                split_lo(C_WO + j0 + 2, 0, m)
                residual(j, C_WO + j0, (sem["wo_res"], j + 1))
                split_lo(C_WO + j0 + 2, 1, m)
                dve.wait_ge(sem["m_hi"], j + 1)
                dve.scalar_tensor_tensor(out=xs[:, j, TOK + META:], in0=res[:, j, :], scalar=gain(G_MLP + j),
                                         in1=xs[:, j, META:TOK].bitcast(F32), op0=ALU.mult,
                                         op1=ALU.subtract).then_inc(sem["m_lo"], 1)

            with dve.Fori(0, KT // 4) as i:
                for j in range(4):
                    wo_block(4 * i + j, j, 4 * i)

            for half in range(2):
                c0, b0, w0 = C_MLP + half * C_HALF, C_MLP + half * B_HALF, W_MLP + half * B_HALF

                def up(n, j0, m=0, root=False):
                    split_lo(c0 + j0 + 2, 0, m)
                    sum_ab(z[:], b0 + j0, w0 + j0, m).then_inc(sem["acc_read"], 1)
                    if root:
                        dve.wait_ge(sem["h_sd"], 1)
                        dve.reciprocal(rstd[:], rstd[:]).then_inc(sem["h_rstd"], 1)
                        dve.wait_ge(sem["h_rstd"], 1)
                    dve.wait_ge(sem["acc_read"], b0 + j0 + 1 + m)
                    dve.scalar_tensor_tensor(out=r[:], in0=z[:], scalar=0.0, in1=rstd[:], op0=ALU.max,
                                             op1=ALU.mult).then_inc(sem["up_r"], 1)
                    split_lo(c0 + j0 + 2, 1, m)
                    dve.wait_ge(sem["up_hi"], n + 1 + half * HALF_F)
                    tt(hid[:, n, FRAMES:], sq[:], hid[:, n, 0:FRAMES].bitcast(F32), ALU.subtract).then_inc(sem["up_lo"], 1)

                for j in range(4):
                    up(j, j, root=half == 0 and j == 0)
                with dve.Fori(1, HALF_F // 4) as i:
                    for j in range(4):
                        up(4 * i + j, j, 4 * i)

                cd, bd = c0 + HALF_F, b0 + HALF_F

                def down(n, j0, m=0, ahead=True):
                    c = cd + 2 * j0
                    if ahead:
                        split_lo(c + 2, 0, m)
                        split_lo(c + 2, 1, m)
                        split_lo(c + 3, 0, m)
                    residual(n, bd + j0, (sem["dn_res"], n + 1 + half * KT))
                    if ahead:
                        split_lo(c + 3, 1, m)

                with dve.Fori(0, KT // 2 - 1) as i:
                    for j in range(2):
                        down(2 * i + j, j, 4 * i)
                down(KT - 2, 0, 4 * (KT // 2 - 1), True)
                down(KT - 1, 1, 4 * (KT // 2 - 1), half == 0)

            dve.wait_ge(sem["fin_sd"], 1)
            dve.reciprocal(rstd[:], z[:]).then_inc(sem["fin_rstd"], 1)
            dve.wait_ge(sem["fin_rstd"], 1)
            for k in range(KT):
                dve.scalar_tensor_tensor(out=res[:, k, :], in0=res[:, k, :], scalar=gain(G_FIN + k), in1=rstd[:],
                                         op0=ALU.mult, op1=ALU.mult).then_inc(sem["fin_out"], 1)

        @block.gpsimd
        def _(pool):
            def tt(o, a, b, op):
                return pool.tensor_tensor(o, a, b, op)

            pool.memset(v_sb[:, 0, :], 0.0).then_inc(sem["meta_pad"], 1)
            pool.memset(pt_m[:], 0.0).then_inc(sem["meta_pad"], 1)
            pool.memset(ret_s[:, FRAMES + P:], 0.0).then_inc(sem["meta_pad"], 1)
            pool.memset(sum_sq[:], 0.0).then_inc(sem["meta_pad"], 1)
            for n in range(4):
                pool.wait_ge(x_part[n], 16)
            tt(x_sq[:], x_in[:], x_in[:], ALU.mult).then_inc(sem["ssx"], 1)
            n = KT // 2
            step = 1
            while n:
                pool.wait_ge(sem["ssx"], step)
                tt(x_sq[:, 0:n, :], x_sq[:, 0:n, :], x_sq[:, n:2 * n, :], ALU.add).then_inc(sem["ssx"], 1)
                n //= 2
                step += 1

            def q_cos(h, c, m):
                pool.wait_ge(sem["acc_read"], c + 1 + m)
                tt(rq[:], zq[:], cos_r[:, META:], ALU.mult).then_inc(sem["rq_cos"], 1)

            def k_cos(h, c, m):
                pool.wait_ge(sem["acc_read"], c + 1 + m)
                tt(rk[:], zk[:], cos_r, ALU.mult).then_inc(sem["rk_cos"], 1)

            def qr_cos(h):
                pool.wait_ge(sem["qr_raw"], h + 1)
                tt(qr[0:ROPE, :], qr_z[0:ROPE, :], consts[0:ROPE, K_COSM + META:K_COSM + TOK], ALU.mult).then_inc(sem["qr_u"], 1)

            def mla_sum(h):
                pool.wait_ge(sem["mla_sq"], h + 1)
                tt(sum_sq[:], sum_sq[:], t2[:], ALU.add).then_inc(sem["mla_ss"], 1)

            def gate_norm(g, c, m):
                pool.wait_ge(sem["acc_read"], c + 1 + m)
                tt(gate_z[:], gate_z[:], rstdx[:, META:], ALU.mult).then_inc(sem["gate_z"], 1)

            def gate_mul(g):
                pool.wait_ge(sem["gate_inv"], g + 1)
                tt(gate[:], gate_z[:], gate[:], ALU.mult).then_inc(sem["gate"], 1)

            pool.wait_ge(sem["cq_lo"], QL // P)
            pool.memset(ret_v[:, 0, :], 0.0).then_inc(sem["meta_pad"], 1)
            pool.wait_ge(sem["tables"], 2)
            q_cos(0, C_HEAD0, 0)
            qr_cos(0)
            k_cos(0, C_HEAD0 + 1, 0)
            pool.wait_ge(sem["meta_pad"], 5)
            mla_sum(0)
            with pool.Fori(0, HEADS - 1) as i:
                c, m, h = C_HEAD, 4 * i, i + 1
                gate_norm(h - 1, c, m)
                qr_cos(h)
                gate_mul(h - 1)
                q_cos(h, c + 1, m)
                k_cos(h, c + 2, m)
                mla_sum(h)
            gate_norm(HEADS - 1, C_GATE7, 0)
            gate_mul(HEADS - 1)

            def res_sum(n, w, wm, done):
                pool.wait_ge(sem["half_b"], w + 1 + wm)
                tt(t2[:], half_b[w % 2][:], res[:, n, :], ALU.add).then_inc(done, 1)

            pool.wait_ge(sem["mla_ss_ps"], 1)
            pool.memset(sum_sq[:], 0.0).then_inc(sem["meta_pad"], 1)
            pool.wait_ge(sem["meta_pad"], 6)
            pool.wait_ge(sem["x_back"], 16)
            with pool.Fori(0, KT // 4) as i:
                for j in range(4):
                    res_sum(4 * i + j, W_WO + j, 4 * i, sem["wo_res"])
                    pool.wait_ge(sem["h_sq"], 4 * i + j + 1)
                    tt(sum_sq[:], sum_sq[:], sq[:], ALU.add).then_inc(sem["h_ss"], 1)
            for half in range(2):
                w0 = W_MLP + half * B_HALF + HALF_F
                pool.wait_ge(sem["h_ss_ps"] if half == 0 else sem["dn_ss"], 1 if half == 0 else KT)
                pool.memset(sum_sq[:], 0.0).then_inc(sem["meta_pad"], 1)
                pool.wait_ge(sem["meta_pad"], 7 + half)
                with pool.Fori(0, KT // 2) as i:
                    for j in range(2):
                        n = 2 * i + j
                        res_sum(n, w0 + j, 2 * i, sem["dn_res"])
                        pool.wait_ge(sem["dn_sq"], n + 1 + half * KT)
                        tt(sum_sq[:], sum_sq[:], sq[:], ALU.add).then_inc(sem["dn_ss"], 1)


def constants():
    f = np.float32
    c = np.zeros((P, K_END), f)
    c[:, K_ID:K_ID + P] = np.eye(P)
    c[:, K_CEN:K_CEN + P] = np.eye(P) - 1.0 / P
    c[:, K_ONE:K_ONE + P] = 1.0
    frame = np.arange(FRAMES)
    meta = np.arange(-META, 0)

    def distance(keys, queries):
        k, q = keys[:, None], queries[None, :]
        seen = k // CHUNK <= q // CHUNK
        return np.where(seen, np.abs(q - k), 1e6).astype(f)

    c[:, K_DIST:K_DIST + FRAMES] = distance(frame[:P], frame)
    c[:, K_DIST + FRAMES:K_DIST + FRAMES + P] = distance(frame[P:], frame[P:])
    c[:META, K_DIST + FRAMES + P:K_DIST + 640] = distance(meta, frame)
    tokens = np.concatenate([meta, frame])

    def additive(queries, keys):
        seen = keys[None, :] // CHUNK <= queries[:, None] // CHUNK
        return np.where(seen, 0.0, -3e38).astype(f)

    c[:, K_MASK:K_MASK + Q0K] = additive(frame[:P], tokens[:Q0K])
    c[:, K_MASK + Q0K:K_MASK + SCORES] = additive(frame[P:], tokens)
    c[:, K_LG:K_LG + HEADS] = np.log(f(1) - f(2) ** (f(-5) - np.arange(HEADS, dtype=f)))[None]
    pos = np.arange(TOK, dtype=f)

    def angles(dim):
        inv = f(1) / (f(10000.0) ** (np.arange(0, dim, 2, dtype=f) / f(dim)))
        return (pos[:, None] * inv[None, :]).astype(f).T

    a = angles(HD)
    c[:, K_COSR:K_COSR + TOK] = np.concatenate([np.cos(a), np.cos(a)])
    c[:, K_SINR:K_SINR + TOK] = np.concatenate([-np.sin(a), np.sin(a)])
    a = angles(ROPE)
    c[:, K_COSM:K_COSM + TOK] = np.concatenate([np.cos(a)] * 4)
    c[:, K_SINM:K_SINM + TOK] = np.concatenate([-np.sin(a), np.sin(a)] * 2)
    c[:, K_EPS] = EPS
    return c


def blocks(w):
    k, n = w.shape
    return w.reshape(k // P, P, n // P, P).transpose(2, 1, 0, 3).reshape(n // P, P, k)


def rows(w):
    return w.reshape(-1, P, w.shape[1]).transpose(1, 0, 2)


def swapped(w):
    return np.concatenate([w[:, w.shape[1] // 2:], w[:, :w.shape[1] // 2]], 1)


def kernel(x, meta_tokens, norm_mix_g, w_in, ret_out_g, q_norm_g, w_uq, kv_norm_g, w_uk, w_uv, mla_out_g, w_o,
           norm_mlp_g, w_up, w_down, final_norm_g):
    import concourse.bacc as bacc
    from concourse.bass_utils import run_bass_kernel_spmd as run

    a = np.asarray
    w = a(w_in)[0]
    ends = np.cumsum([HEADS * HD] * 4 + [QL, KVL, ROPE])
    wq, wk, wv, wg, wcq, wckv, wkr = np.split(w, ends[:-1], axis=1)
    bq, bk, bv, bg = (blocks(m) for m in (wq, wk, wv, wg))
    order = [blocks(wcq), blocks(wckv), blocks(np.concatenate([wkr, swapped(wkr)], 1)), bq[0:1], bk[0:1], bv[0:1]]
    for h in range(1, HEADS):
        order += [bg[h - 1:h], bq[h:h + 1], bk[h:h + 1], bv[h:h + 1]]
    stream_in = np.concatenate(order + [bg[HEADS - 1:]])

    uq = a(w_uq)[0].reshape(QL, HEADS, NOPE + ROPE)
    uk = a(w_uk)[0].reshape(KVL, HEADS, NOPE)
    uv = a(w_uv)[0].reshape(KVL, HEADS, HD)

    def side_of(h):
        rot = uq[:, h, NOPE:]
        parts = [uq[:, h, :NOPE], np.concatenate([rot, swapped(rot)], 1), uk[:, h], uv[:, h]]
        return np.concatenate([rows(m).reshape(P, -1) for m in parts], 1)

    side = np.stack([side_of(h) for h in range(HEADS)])
    up = blocks(a(w_up)[0])
    half = DFF // 2
    down = a(w_down)[0].reshape(2, DOWN_PER_BLOCK, D, D)
    down = np.stack([np.stack([blocks(down[i, j]) for j in range(DOWN_PER_BLOCK)], 1) for i in range(2)])
    down = down.reshape(-1, P, W)
    frames = rows(a(x)[0].T)
    tokens = np.concatenate([rows(a(meta_tokens).T), frames], 2)
    g = [a(norm_mix_g)[0], a(q_norm_g)[0], a(kv_norm_g)[0], a(ret_out_g)[0], a(mla_out_g)[0], a(norm_mlp_g)[0],
         a(final_norm_g)]
    gains = np.concatenate([v.reshape(-1, P).T for v in g], 1)

    ins = {"w_in": stream_in, "w_side": side, "w_o": blocks(a(w_o)[0]), "w_up": up, "w_down": down,
           "x_all": tokens, "x_frames": frames, "gains_in": gains, "consts_in": constants()}
    ins = {n: np.ascontiguousarray(v) for n, v in ins.items()}
    nc = bacc.Bacc("TRN2", target_bir_lowering=False, num_devices=1)
    aps = {n: nc.dram_tensor(n, v.shape, mybir.dt.from_np(v.dtype), kind="ExternalInput").ap() for n, v in ins.items()}
    aps["out"] = nc.dram_tensor("out", (P, KT, FRAMES), F32, kind="ExternalOutput").ap()
    hymba_block(nc, **aps)
    got = run(nc, [ins], core_ids=[0]).results[0]["out"]
    return got.transpose(1, 0, 2).reshape(D, FRAMES).T.reshape(1, FRAMES, D)
```

```python
from contextlib import ExitStack

import numpy as np

import concourse.bass as bass
from concourse import mybir

F32 = mybir.dt.float32
F32R = mybir.dt.float32r
ALU = mybir.AluOpType
ACT = mybir.ActivationFunctionType
AX = mybir.AxisListType

P = 128
D = 2048
FRAMES = 256
META = 16
TOK = META + FRAMES
CHUNK = 64
HEADS = 8
HD = 128
NOPE, ROPE = 128, 64
QL, KVL = 512, 256
DFF = 8192
EPS = 1e-6
KT = D // P
W = KT * P
RAWS = 4

C_KV, C_CQ, C_KR, C_HEAD0 = 0, 2, 6, 7
C_HEAD = C_HEAD0 + 3
C_GATE7 = C_HEAD + 4 * (HEADS - 1)
C_WO = C_GATE7 + 1
C_MLP = C_WO + KT
HALF_F = DFF // P // 2
DOWN_PER_BLOCK = HALF_F // KT
C_HALF = HALF_F + DOWN_PER_BLOCK * KT
B_HALF = HALF_F + KT
W_HEAD0 = 4
W_HEAD = 5
W_GATE7 = W_HEAD + 2 * (HEADS - 1)
W_WO = W_GATE7 + 1
W_MLP = W_WO + KT
C_END = C_MLP + 2 * C_HALF

WO_ORDER = [*range(HEADS - 1), *range(HEADS, 2 * HEADS), HEADS - 1]

SIDE_Q, SIDE_R, SIDE_K, SIDE_V, SIDE_END = 0, 512, 1024, 1280, 1536
K_ID, K_CEN, K_ONE, K_DIST, K_MASK, K_LG, K_COSR, K_SINR, K_COSM, K_SINM, K_EPS = (
    0, 128, 256, 384, 1024, 1440, 1448, 1720, 1992, 2264, 2536)
K_END = 2537
G_MIX, G_Q, G_KV, G_RET, G_MLA, G_MLP, G_FIN = 0, 16, 20, 22, 30, 38, 54
G_END = 70
F0, F1 = META, META + P
Q0K, Q1K = META + P, TOK
SCORES = Q0K + Q1K

EVENTS = """hi_ready lo_ready chunk_used acc_read half_b
x_hi x_lo meta_pad ssx ss_x_ps ss_q_ps ss_k_ps rx_sd rstdx cq_raw cq_sq cq_sum cq_sd cq_scaled cq_hi cq_lo cq_var kv_var
kv_raw kv_sq kv_sum kv_sd kv_scaled kv_hi kv_lo kr_raw kr_ready tables stat
side_hi side_lo qn_ps qr_ps kn_ps v_ps qn_b qr_b qn_raw qn_ready qr_raw qr_ready qr_u kn_ready v_ready
mla_s_ps mla_s mla_max mla_exp mla_inv mla_p pt_ps pt_m pt_f mla_o_ps mla_o mla_sq mla_ss mla_ss_ps mla_sd
mla_rstd mla_a mla_hi mla_lo
rq_raw rq_sw rq_cos rq_sin rq_ready rk_raw rk_cos rk_sin rk_ready decay ret_s_ps ret_y_ps ret_s ret_v
ret_o_ps ret_o cen_ps cen ret_sq var_ps ret_sd ret_inv ret_y ret_a ret_hi ret_lo
gate_raw gate_z gate_exp gate_den gate_inv gate
x_back wo_res h_ready m_hi m_lo h_sq h_ss h_ss_ps h_sd h_rstd
up_z up_r up_sq up_hi up_lo dn_res dn_h dn_sq dn_ss fin_ps fin_sd fin_rstd fin_out fin_g fin_pool last_a stored
side_landed first_half gains_landed consts_landed""".split()


def hymba_block(nc, w_in, w_side, w_o, w_up, w_down, x_all, x_frames, gains_in, consts_in, out):
    ctx = ExitStack()
    with ctx:
        sem = {n: ctx.enter_context(nc.semaphore(n)) for n in EVENTS}
        raw_landed = [ctx.enter_context(nc.semaphore(f"raw_landed{i}")) for i in range(RAWS)]
        x_part = [ctx.enter_context(nc.semaphore(f"x_part{i}")) for i in range(4)]

        at = (nc.sbuf_base + 31) // 32 * 32
        arena = ctx.enter_context(nc.sbuf_tensor("arena", [P, (nc.sbuf_usable_end - at) // 4 - 16], F32))
        here = [at]

        def place(name, shape, dt=F32):
            t = nc.alloc_sbuf_tensor_at(name, [P] + shape, dt, offset=here[0])
            size = 4
            for n in shape:
                size *= n
            here[0] += (size + 31) // 32 * 32
            return t

        raw = [place(f"raw{i}", [W]) for i in range(RAWS)]
        hi = [place(f"hi{i}", [W], F32R) for i in range(2)]
        lo = [place(f"lo{i}", [W], F32R) for i in range(2)]
        xs = place("xs", [KT, 2 * TOK], F32R)
        hid_at = here[0]
        hid = place("hid", [HALF_F, 2 * FRAMES], F32R)
        res_at = here[0]
        res = place("res", [KT, FRAMES])
        half_b = [place(f"half_b{i}", [FRAMES]) for i in range(2)]
        gains = place("gains", [G_END])
        consts = place("consts", [K_END])
        rstdx = place("rstdx", [TOK])
        sum_sq = place("sum_sq", [FRAMES])
        rstd = place("rstd", [FRAMES])
        sq = place("sq", [FRAMES])
        z = place("z", [FRAMES])
        r = place("r", [FRAMES])
        t2 = place("t2", [FRAMES])
        rest_at = here[0]

        here[0] = hid_at + 2 * KT * TOK * 4
        mla_o = place("mla_o", [HEADS, FRAMES])
        cq = place("cq", [QL // P, FRAMES])
        cqs = place("cqs", [QL // P, 2 * FRAMES], F32R)
        ckv = place("ckv", [KVL // P, TOK])
        ckvs = place("ckvs", [KVL // P, 2 * TOK], F32R)
        kr = place("kr", [TOK])
        assert here[0] <= res_at
        here[0] = hid_at + (2 * KT * TOK + HEADS * FRAMES) * 4
        decay = place("decay", [640])
        ret_v = place("ret_v", [3, P])
        here[0] = hid_at
        x_in = place("x_in", [KT, TOK])
        x_sq = place("x_sq", [KT, TOK])
        here[0] = hid_at + HEADS * 2 * FRAMES * 4
        side = place("side", [SIDE_END])
        side_hi = place("side_hi", [SIDE_V], F32R)
        zk = place("zk", [TOK])
        swk = place("swk", [TOK])
        zq = place("zq", [FRAMES])
        swq = place("swq", [FRAMES])
        rq = place("rq", [FRAMES])
        assert here[0] <= hid_at + 2 * KT * TOK * 4
        here[0] = res_at
        qn = place("qn", [FRAMES])
        qn_b = place("qn_b", [FRAMES])
        qr_b = place("qr_b", [FRAMES])
        qr_z = place("qr_z", [FRAMES])
        qr_v = place("qr_v", [FRAMES])
        qr = place("qr", [FRAMES])
        kn = place("kn", [TOK])
        pt_f = place("pt_f", [3, P])
        probs = place("probs", [SCORES])
        gate_z = place("gate_z", [FRAMES])
        rk = place("rk", [TOK])
        rv = place("rv", [TOK])
        assert here[0] <= res_at + (KT * FRAMES - 5 * P) * 4
        assert here[0] <= res_at + KT * FRAMES * 4
        here[0] = res_at
        cq_sq = place("cq_sq", [QL // P, FRAMES])
        kv_sq = place("kv_sq", [KVL // P, TOK])
        rx_sd = place("rx_sd", [TOK])
        rstdx2 = place("rstdx2", [TOK])
        cq_var = place("cq_var", [FRAMES])
        cq_ss = place("cq_ss", [FRAMES])
        cq_sd = place("cq_sd", [FRAMES])
        kv_var = place("kv_var", [TOK])
        kv_f = place("kv_f", [TOK])
        kr_v = kv_sq[:, 1, :]
        v_sb = place("v_sb", [3, P])
        pt_m = place("pt_m", [FRAMES])
        assert here[0] <= res_at + KT * FRAMES * 4
        here[0] = rest_at
        side_lo = place("side_lo", [SIDE_V], F32R)
        ret_s = place("ret_s", [640])
        q_rstd = place("q_rstd", [FRAMES])
        cen = place("cen", [FRAMES])
        gate = place("gate", [FRAMES])
        stats = place("stats", [8])

        assert here[0] <= nc.sbuf_usable_end

        def bank(name):
            return ctx.enter_context(nc.psum_tensor(name, [P, 512], F32))

        acc = [bank(f"acc{i}") for i in range(2)]
        ps_qn, ps_qr, ps_kn, ps_v, ps_x, ps_y = (bank(n) for n in ("ps_qn", "ps_qr", "ps_kn", "ps_v", "ps_x", "ps_y"))

        ident = consts[:, K_ID:K_ID + P]
        center = consts[:, K_CEN:K_CEN + P]
        ones = consts[:, K_ONE:K_ONE + P]
        dist = consts[:, K_DIST:K_DIST + 640]
        mask = consts[:, K_MASK:K_MASK + SCORES]
        cos_r = consts[:, K_COSR:K_COSR + TOK]
        sin_r = consts[:, K_SINR:K_SINR + TOK]
        cos_q = consts[0:ROPE, K_COSM + META:K_COSM + TOK]
        sin_q = consts[ROPE:, K_SINM + META:K_SINM + TOK]
        eps = consts[:, K_EPS:K_EPS + 1]

        def gain(col):
            return gains[:, bass.ds(col, 1)]

        def halves(t, c, part):
            return t[c % 2][:, part * W // 2:(part + 1) * W // 2]

        def raw_half(c, part):
            return raw[c % RAWS][:, part * W // 2:(part + 1) * W // 2]

        block = ctx.enter_context(nc.Block())

        @block.sync
        def _(sp):
            def load(src, c, more=0):
                if c >= RAWS:
                    sp.wait_ge(sem["lo_ready"], 2 * (c - RAWS) + 2 + 2 * more)
                sp.dma_start(raw[c % RAWS][:], src).then_inc(raw_landed[c % RAWS], 16)

            sp.dma_start(gains[:], gains_in).then_inc(sem["gains_landed"], 16)
            sp.dma_start(x_in[:, 0:4, :], x_all[:, 0:4, :]).then_inc(x_part[0], 16)
            sp.dma_start(raw[0][:, 0:W // 2], w_in[0, :, 0:W // 2]).then_inc(sem["first_half"], 16)
            sp.dma_start(x_in[:, 4:8, :], x_all[:, 4:8, :]).then_inc(x_part[1], 16)
            sp.dma_start(raw[0][:, W // 2:], w_in[0, :, W // 2:]).then_inc(raw_landed[0], 16)
            for n in range(2, 4):
                sp.dma_start(x_in[:, 4 * n:4 * n + 4, :], x_all[:, 4 * n:4 * n + 4, :]).then_inc(x_part[n], 16)
            load(w_in[1], 1)
            sp.dma_start(consts[:], consts_in).then_inc(sem["consts_landed"], 16)
            load(w_in[2], 2)
            load(w_in[3], 3)
            with sp.Fori(0, 8) as i:
                for j in range(4):
                    load(w_in[4 * i + 4 + j], 4 + j, 4 * i)
            for c in range(36, C_WO):
                load(w_in[c], c)
            for j in range(4):
                load(w_o[j], C_WO + j)
            sp.wait_ge(sem["mla_o"], HEADS)
            sp.wait_ge(sem["gate"], HEADS)
            sp.wait_ge(sem["ret_v"], 2 * HEADS)
            sp.dma_start(res[:], x_frames).then_inc(sem["x_back"], 16)
            with sp.Fori(1, KT // 4) as i:
                for j in range(4):
                    load(w_o[4 * i + j], C_WO + j, 4 * i)
            for half in range(2):
                with sp.Fori(0, HALF_F // 4) as i:
                    for j in range(4):
                        load(w_up[4 * i + half * HALF_F + j], C_MLP + half * C_HALF + j, 4 * i)
                with sp.Fori(0, HALF_F // 4) as i:
                    for j in range(4):
                        load(w_down[4 * i + half * HALF_F + j], C_MLP + half * C_HALF + HALF_F + j, 4 * i)
            for q in range(4):
                sp.wait_ge(sem["fin_out"], 3 * q + 3)
                sp.wait_ge(sem["fin_pool"], q + 1)
                sp.dma_start(out[:, 4 * q:4 * q + 4, :], res[:, 4 * q:4 * q + 4, :]).then_inc(sem["stored"], 16)
            sp.wait_ge(sem["stored"], 64)

        @block.tensor
        def _(pe):
            def mm(o, l, m, start=True, stop=True):
                return pe.matmul(o, l, m, start=start, stop=stop)

            def wide(c, b, wide_of, hi_of, more=0, bmore=0, first=True, last=True, order=None, ready=None):
                a = acc[b % 2]
                order = order or list(range(KT))
                for n, k in enumerate(order):
                    if n % 8 == 0:
                        pe.wait_ge(sem["lo_ready"], 2 * c + n // 8 + 1 + 2 * more)
                    if n == 0 and first and b >= 2:
                        pe.wait_ge(sem["acc_read"], b - 1 + bmore)
                    if ready is not None:
                        ready(k)
                    wh = hi[c % 2][:, k * P:k * P + P]
                    wl = lo[c % 2][:, k * P:k * P + P]
                    end = last and n == KT - 1
                    if end:
                        mm(a[:, FRAMES:], wl, hi_of(k), False, False)
                    m = mm(a[:].rearrange("p (a t) -> p a t", a=2), wh, wide_of(k), first and n == 0, end)
                    if not end:
                        m = mm(a[:, FRAMES:], wl, hi_of(k), False, False)
                    if n % 8 == 7:
                        m.then_inc(sem["chunk_used"], 1)

            def x_wide(k):
                return xs[:, k, :].rearrange("p (a t) -> p a t", a=2)[:, :, META:]

            def x_hi(k):
                return xs[:, k, META:TOK]

            def narrow(c, more=0, ready=None):
                a = acc[c % 2][:, 0:TOK]
                for k in range(KT):
                    if k % 8 == 0:
                        pe.wait_ge(sem["lo_ready"], 2 * c + k // 8 + 1 + 2 * more)
                    if k == 0 and c >= 2:
                        pe.wait_ge(sem["acc_read"], c - 1 + more)
                    if ready is not None:
                        ready(k)
                    wh = hi[c % 2][:, k * P:k * P + P]
                    wl = lo[c % 2][:, k * P:k * P + P]
                    mm(a, wl, xs[:, k, 0:TOK], k == 0, False)
                    mm(a, wh, xs[:, k, TOK:], False, False)
                    m = mm(a, wh, xs[:, k, 0:TOK], False, k == KT - 1)
                    if k % 8 == 7:
                        m.then_inc(sem["chunk_used"], 1)

            def mla_project(h, first=False):
                if first:
                    pe.wait_ge(sem["cq_lo"], 4)
                    pe.wait_ge(sem["kv_lo"], 1)
                else:
                    pe.wait_ge(sem["mla_o"], h)
                pe.wait_ge(sem["side_lo"], h + 1)
                for (o, col, done) in ((ps_qn, SIDE_Q, sem["qn_ps"]), (ps_qr, SIDE_R, sem["qr_ps"])):
                    for k in range(QL // P):
                        wh = side_hi[:, col + k * P:col + (k + 1) * P]
                        wl = side_lo[:, col + k * P:col + (k + 1) * P]
                        end = k == QL // P - 1
                        if end:
                            mm(o[:, FRAMES:], wl, cqs[:, k, 0:FRAMES], False, False)
                        m = mm(o[:], wh, cqs[:, k, :], k == 0, end)
                        if not end:
                            mm(o[:, FRAMES:], wl, cqs[:, k, 0:FRAMES], False, False)
                    m.then_inc(done, 1)
                for k in range(KVL // P):
                    wh = side_hi[:, SIDE_K + k * P:SIDE_K + (k + 1) * P]
                    wl = side_lo[:, SIDE_K + k * P:SIDE_K + (k + 1) * P]
                    mm(ps_kn[:, 0:TOK], wl, ckvs[:, k, 0:TOK], k == 0, False)
                    mm(ps_kn[:, 0:TOK], wh, ckvs[:, k, TOK:], False, False)
                    m = mm(ps_kn[:, 0:TOK], wh, ckvs[:, k, 0:TOK], False, k == KVL // P - 1)
                m.then_inc(sem["kn_ps"], 1)
                for n, (t0, tn) in enumerate(((0, META), (F0, P), (F1, P))):
                    for k in range(KVL // P):
                        m = mm(ps_v[0:tn, n * P:n * P + P], ckv[:, k, t0:t0 + tn],
                               side[:, SIDE_V + k * P:SIDE_V + (k + 1) * P], k == 0, k == KVL // P - 1)
                m.then_inc(sem["v_ps"], 1)

            def mla_scores(h):
                pe.wait_ge(sem["qn_ready"], h + 1)
                pe.wait_ge(sem["kn_ready"], h + 1)
                pe.wait_ge(sem["qr_ready"], h + 1)
                for n, (c0, keys) in enumerate(((0, Q0K), (Q0K, Q1K))):
                    mm(ps_qn[:, c0:c0 + keys], qn[:, n * P:n * P + P], kn[:, 0:keys], True, False)
                    m = mm(ps_qn[:, c0:c0 + keys], qr[0:ROPE, n * P:n * P + P], kr[0:ROPE, 0:keys], False, True)
                m.then_inc(sem["mla_s_ps"], 1)

            def mla_turn(h):
                pe.wait_ge(sem["mla_p"], 2 * h + 2)
                pe.wait_ge(sem["v_ready"], 2 * h + 2)
                for n, c0 in enumerate((0, Q0K)):
                    pe.transpose(ps_v[0:META, n * P:n * P + P], probs[:, c0:c0 + META], ident)
                    pe.transpose(ps_kn[:, n * P:n * P + P], probs[:, c0 + F0:c0 + F0 + P], ident)
                pe.transpose(ps_kn[:, 2 * P:3 * P], probs[:, Q0K + F1:Q0K + F1 + P], ident).then_inc(sem["pt_ps"], 1)

            def mla_values(h):
                pe.wait_ge(sem["pt_f"], h + 1)
                pe.wait_ge(sem["pt_m"], h + 1)
                mm(ps_qn[:, 0:FRAMES], v_sb[:, 1, :], pt_f[:, 0:2, :].rearrange("p a t -> p (a t)"), True, False)
                mm(ps_qn[:, P:FRAMES], v_sb[:, 2, :], pt_f[:, 2, :], False, False)
                mm(ps_qn[:, 0:FRAMES], v_sb[:, 0, :], pt_m[:], False, True).then_inc(sem["mla_o_ps"], 1)

            def ret_scores(g, first=False):
                pe.wait_ge(sem["rq_ready"], g + 1)
                pe.wait_ge(sem["rk_ready"], g + 1)
                pe.wait_ge(sem["acc_read"], C_HEAD + 4 * g)
                if not first:
                    pe.wait_ge(sem["ret_sd"], g)
                mm(ps_x[:, 0:FRAMES], rk[:, F0:F0 + P], rq[:])
                mm(ps_x[0:META, FRAMES:], rk[:, 0:META], rq[:]).then_inc(sem["ret_s_ps"], 1)
                mm(ps_y[:, 0:P], rk[:, F1:F1 + P], rq[:, P:])
                mm(ps_y[0:META, P:2 * P], rv[:, 0:META], center)
                mm(ps_y[:, 2 * P:3 * P], rv[:, F0:F0 + P], center)
                mm(ps_y[:, 3 * P:4 * P], rv[:, F1:F1 + P], center).then_inc(sem["ret_y_ps"], 1)

            def ret_values(g):
                pe.wait_ge(sem["ret_s"], 3 * g + 3)
                pe.wait_ge(sem["ret_v"], 2 * g + 2)
                mm(ps_qr[:, 0:FRAMES], ret_v[:, 1, :], ret_s[:, 0:FRAMES], True, False)
                mm(ps_qr[:, P:FRAMES], ret_v[:, 2, :], ret_s[:, FRAMES:FRAMES + P], False, False)
                mm(ps_qr[:, 0:FRAMES], ret_v[:, 0, :], ret_s[:, FRAMES + P:], False, True).then_inc(sem["ret_o_ps"], 1)

            def ret_var(g):
                pe.wait_ge(sem["ret_sq"], g + 1)
                mm(ps_y[:, 0:FRAMES], ones, sq[:]).then_inc(sem["var_ps"], 1)

            def x_parts(k):
                pe.wait_ge(sem["x_lo"], k + 1)

            narrow(0, ready=x_parts)
            narrow(1)
            wide(2, 2, x_wide, x_hi)
            wide(3, 3, x_wide, x_hi)
            pe.wait_ge(sem["consts_landed"], 16)
            pe.wait_ge(sem["ssx"], 5)
            mm(ps_x[:, 0:TOK], ones, x_sq[:, 0, :]).then_inc(sem["ss_x_ps"], 1)
            pe.wait_ge(sem["kv_sum"], 1)
            mm(ps_v[:, 0:TOK], ones, kv_sq[:, 0, :]).then_inc(sem["ss_k_ps"], 1)
            wide(4, 4, x_wide, x_hi)
            wide(5, 5, x_wide, x_hi)
            narrow(6)
            pe.wait_ge(sem["cq_sum"], QL // P)
            mm(ps_y[:, 0:FRAMES], ones, cq_ss[:]).then_inc(sem["ss_q_ps"], 1)

            wide(C_HEAD0, C_HEAD0, x_wide, x_hi)
            mla_project(0, True)
            narrow(C_HEAD0 + 1)
            mla_scores(0)
            narrow(C_HEAD0 + 2)
            mla_turn(0)
            mla_values(0)

            def head(h, i, first=False):
                c = C_HEAD
                m = 4 * i
                wide(c, c, x_wide, x_hi, m, m)
                mla_project(h)
                ret_scores(h - 1, first)
                wide(c + 1, c + 1, x_wide, x_hi, m, m)
                mla_scores(h)
                ret_values(h - 1)
                narrow(c + 2, m)
                mla_turn(h)
                ret_var(h - 1)
                narrow(c + 3, m)
                mla_values(h)

            head(1, 0, True)
            with pe.Fori(1, HEADS - 1) as i:
                head(i + 1, i)

            wide(C_GATE7, C_GATE7, x_wide, x_hi)
            pe.wait_ge(sem["mla_ss"], HEADS)
            mm(ps_kn[:, 0:FRAMES], ones, sum_sq[:]).then_inc(sem["mla_ss_ps"], 1)
            ret_scores(HEADS - 1)

            def hid_wide(k):
                return hid[:, k, :].rearrange("p (a t) -> p a t", a=2)

            def hid_hi(k):
                return hid[:, k, 0:FRAMES]

            def wo_block(c, more=0):
                wide(c, c, lambda k: hid_wide(WO_ORDER[k]), lambda k: hid_hi(WO_ORDER[k]), more, more)

            def mixed(k):
                tile = WO_ORDER[k]
                if tile == HEADS:
                    ret_values(HEADS - 1)
                if tile == HEADS + 3:
                    ret_var(HEADS - 1)
                if tile < HEADS:
                    pe.wait_ge(sem["ret_lo"], tile + 1)
                else:
                    pe.wait_ge(sem["mla_lo"], tile - HEADS + 1)

            wide(C_WO, C_WO, lambda k: hid_wide(WO_ORDER[k]), lambda k: hid_hi(WO_ORDER[k]), ready=mixed)
            for j in range(1, 4):
                wo_block(C_WO + j)
            with pe.Fori(1, KT // 4) as i:
                for j in range(4):
                    wo_block(C_WO + j, 4 * i)

            for half in range(2):
                c0, b0 = C_MLP + half * C_HALF, C_MLP + half * B_HALF

                def m_parts(k):
                    pe.wait_ge(sem["m_lo"], k + 1)

                def up(j, more=0, ready=None):
                    wide(c0 + j, b0 + j, x_wide, x_hi, more, more, ready=ready)

                up(0, ready=m_parts if half == 0 else None)
                if half == 0:
                    pe.wait_ge(sem["h_ss"], KT)
                    mm(ps_x[:, 0:FRAMES], ones, sum_sq[:]).then_inc(sem["h_ss_ps"], 1)
                for j in range(1, 4):
                    up(j)
                with pe.Fori(1, HALF_F // 4) as i:
                    for j in range(4):
                        up(j, 4 * i)

                cd, bd = c0 + HALF_F, b0 + HALF_F

                def down(n, more=0, bmore=0, guard=False):
                    for part in range(DOWN_PER_BLOCK):
                        def up_parts(k, part=part):
                            pe.wait_ge(sem["up_lo"], half * HALF_F + part * KT + k + 1)
                        wide(cd + DOWN_PER_BLOCK * n + part, bd + n, lambda k: hid_wide(part * KT + k),
                             lambda k: hid_hi(part * KT + k), more, bmore, first=part == 0,
                             last=part == DOWN_PER_BLOCK - 1, ready=up_parts if guard else None)

                down(0, guard=True)
                down(1)
                with pe.Fori(1, KT // 2) as i:
                    down(0, 4 * i, 2 * i)
                    down(1, 4 * i, 2 * i)

            pe.wait_ge(sem["dn_ss"], 2 * KT - 1)
            mm(ps_x[:, 0:FRAMES], ones, sum_sq[:], True, False)
            pe.wait_ge(sem["dn_sq"], 2 * KT)
            mm(ps_x[:, 0:FRAMES], ones, sq[:], False, True).then_inc(sem["fin_ps"], 1)

        @block.scalar
        def _(act):
            def copy(o, i):
                return act.activation(o, i, ACT.Copy)

            def split_hi(c, part, more=0):
                if c < 0 or c >= C_END:
                    return
                if c == 0 and part == 0:
                    act.wait_ge(sem["first_half"], 16)
                elif part == 0 or c == 0:
                    act.wait_ge(raw_landed[c % RAWS], 16 * (c // RAWS + 1) + 4 * more)
                if c >= 2:
                    act.wait_ge(sem["chunk_used"], 2 * (c - 2) + part + 1 + 2 * more)
                copy(halves(hi, c, part), raw_half(c, part)).then_inc(sem["hi_ready"], 1)

            def b_copy(c, w, more=0):
                act.wait_ge(sem["chunk_used"], 2 * c + 2 + 2 * more)
                return copy(half_b[w % 2][:], acc_of[0][:, FRAMES:]).then_inc(sem["half_b"], 1)

            acc_of = [None]

            def wide_block(c, b, w, more=0, ahead=True):
                acc_of[0] = acc[b % 2]
                if ahead:
                    split_hi(c + 2, 0, more)
                b_copy(c, w, more)
                if ahead:
                    split_hi(c + 2, 1, more)

            def side_load(h):
                act.dma_start(side[:], w_side[h]).then_inc(sem["side_landed"], 16)

            def side_split(h):
                act.wait_ge(sem["side_landed"], 16 * h + 16)
                copy(side_hi[:], side[:, 0:SIDE_V]).then_inc(sem["side_hi"], 1)

            act.wait_ge(sem["gains_landed"], 16)

            def x_round(k):
                act.wait_ge(x_part[k // 4], 16)
                act.activation(xs[:, k, 0:TOK], x_in[:, k, :], ACT.Identity, scale=gain(G_MIX + k)).then_inc(sem["x_hi"], 1)

            for k in range(3):
                x_round(k)
            split_hi(0, 0)
            for k in range(3, 8):
                x_round(k)
            split_hi(0, 1)
            for k in range(8, 16):
                x_round(k)
            split_hi(1, 0)
            split_hi(1, 1)

            for c in range(2):
                split_hi(c + 2, 0)
                split_hi(c + 2, 1)
            act.wait_ge(sem["acc_read"], C_CQ)
            act.activation(kv_sq[:], ckv[:], ACT.Square).then_inc(sem["kv_sq"], 1)

            def cq_block(k):
                wide_block(C_CQ + k, C_CQ + k, k)
                act.wait_ge(sem["acc_read"], C_CQ + k + 1)
                act.activation(cq_sq[:, k, :], cq[:, k, :], ACT.Square).then_inc(sem["cq_sq"], 1)
                act.activation(cqs[:, k, 0:FRAMES], cq[:, k, :], ACT.Identity,
                               scale=gain(G_Q + k)).then_inc(sem["cq_hi"], 1)

            cq_block(0)
            cq_block(1)
            act.wait_ge(sem["ss_x_ps"], 1)
            act.activation(rx_sd[:], ps_x[:, 0:TOK], ACT.Sqrt, bias=eps, scale=1.0 / D).then_inc(sem["rx_sd"], 1)
            act.wait_ge(sem["kv_var"], 1)
            act.activation(kv_f[:], kv_var[:], ACT.Sqrt, bias=eps, scale=1.0 / KVL).then_inc(sem["kv_sd"], 1)
            act.wait_ge(sem["x_lo"], KT)
            side_load(0)
            cq_block(2)
            act.wait_ge(sem["kv_scaled"], 2)
            copy(ckvs[:, :, 0:TOK], ckv[:]).then_inc(sem["kv_hi"], 1)
            cq_block(3)
            split_hi(8, 0)
            act.wait_ge(sem["chunk_used"], 2 * C_KR + 2)
            copy(zk[:], acc[C_KR % 2][:, 0:TOK]).then_inc(sem["acc_read"], 1)
            split_hi(8, 1)
            act.wait_ge(sem["cq_var"], 1)
            act.activation(cq_sd[:], cq_var[:], ACT.Sqrt, bias=eps, scale=1.0 / QL).then_inc(sem["cq_sd"], 1)
            side_split(0)

            def q_block(h, c, w, more):
                wide_block(c, c, w, more)
                act.wait_ge(sem["acc_read"], c + 1 + more)
                copy(swq[0:64, :], zq[64:128, :]).then_inc(sem["rq_sw"], 1)
                copy(swq[64:128, :], zq[0:64, :]).then_inc(sem["rq_sw"], 1)

            def k_block(h, c, more):
                split_hi(c + 2, 0, more)
                act.wait_ge(sem["chunk_used"], 2 * c + 2 + 2 * more)
                a = acc[c % 2]
                copy(zk[:], a[:, 0:TOK])
                copy(swk[0:64, :], a[64:128, 0:TOK])
                copy(swk[64:128, :], a[0:64, 0:TOK]).then_inc(sem["acc_read"], 1)
                split_hi(c + 2, 1, more)

            def v_block(h, c, more):
                split_hi(c + 2, 0, more)
                split_hi(c + 2, 1, more)

            def mla_in(h):
                act.wait_ge(sem["qn_ps"], h + 1)
                copy(qn_b[:], ps_qn[:, FRAMES:]).then_inc(sem["qn_b"], 1)
                act.wait_ge(sem["qr_ps"], h + 1)
                copy(qr_b[:], ps_qr[:, FRAMES:]).then_inc(sem["qr_b"], 1)
                act.wait_ge(sem["v_ps"], h + 1)
                copy(v_sb[0:META, 0, :], ps_v[0:META, 0:P]).then_inc(sem["v_ready"], 1)
                copy(v_sb[:, 1:3, :].rearrange("p a t -> p (a t)"), ps_v[:, P:3 * P]).then_inc(sem["v_ready"], 1)

            def mla_exp(h):
                for n, (c0, keys) in enumerate(((0, Q0K), (Q0K, Q1K))):
                    act.wait_ge(sem["mla_max"], 2 * h + n + 1)
                    act.activation(probs[:, c0:c0 + keys], probs[:, c0:c0 + keys], ACT.Exp, bias=stats[:, n:n + 1],
                                   accum_out=stats[:, 2 + n:3 + n]).then_inc(sem["mla_exp"], 1)

            def mla_turned(h):
                act.wait_ge(sem["pt_ps"], h + 1)
                copy(pt_m[0:META, :], ps_v[0:META, 0:FRAMES]).then_inc(sem["pt_m"], 1)

            def mla_square(h):
                act.wait_ge(sem["mla_o"], h + 1)
                act.activation(t2[:], mla_o[:, h, :], ACT.Square).then_inc(sem["mla_sq"], 1)

            def ret_decay(g, first=False):
                if not first:
                    act.wait_ge(sem["ret_s"], 3 * g)
                act.activation(decay[:], dist, ACT.Exp, scale=consts[:, bass.ds(K_LG + g, 1)]).then_inc(sem["decay"], 1)

            def ret_out(g):
                act.wait_ge(sem["ret_o_ps"], g + 1)
                copy(cen[:], ps_qr[:, 0:FRAMES]).then_inc(sem["cen"], 1)
                act.activation(sq[:], ps_qr[:, 0:FRAMES], ACT.Square).then_inc(sem["ret_sq"], 1)

            def ret_root(g):
                act.wait_ge(sem["var_ps"], g + 1)
                act.activation(z[:], ps_y[:, 0:FRAMES], ACT.Sqrt, bias=eps, scale=1.0 / HD).then_inc(sem["ret_sd"], 1)

            def ret_round(g):
                act.wait_ge(sem["ret_a"], g + 1)
                copy(hid[:, g, 0:FRAMES], cen[:]).then_inc(sem["ret_hi"], 1)

            def gate_exp(g):
                act.wait_ge(sem["gate_z"], g + 1)
                act.activation(gate[:], gate_z[:], ACT.Exp, scale=-1.0).then_inc(sem["gate_exp"], 1)

            q_block(0, C_HEAD0, W_HEAD0, 0)
            mla_in(0)
            k_block(0, C_HEAD0 + 1, 0)
            mla_exp(0)
            act.wait_ge(sem["v_ps"], 1)
            side_load(1)
            v_block(0, C_HEAD0 + 2, 0)
            mla_turned(0)
            mla_square(0)
            side_split(1)

            def head(h, i, first=False, last=False):
                c, m = C_HEAD, 4 * i
                wide_block(c, c, W_HEAD, m)
                ret_decay(h - 1, first)
                mla_in(h)
                gate_exp(h - 1)
                q_block(h, c + 1, W_HEAD + 1, m)
                ret_out(h - 1)
                mla_exp(h)
                if not last:
                    act.wait_ge(sem["v_ps"], h + 1)
                    side_load(h + 1)
                k_block(h, c + 2, m)
                mla_turned(h)
                if not last:
                    side_split(h + 1)
                ret_root(h - 1)
                v_block(h, c + 3, m)
                ret_round(h - 1)
                mla_square(h)

            head(1, 0, True)
            with act.Fori(1, HEADS - 2) as i:
                head(i + 1, i)
            head(HEADS - 1, HEADS - 2, last=True)

            g = HEADS - 1
            wide_block(C_GATE7, C_GATE7, W_GATE7)
            ret_decay(g)
            gate_exp(g)
            act.wait_ge(sem["mla_ss_ps"], 1)
            act.activation(rstd[:], ps_kn[:, 0:FRAMES], ACT.Sqrt, bias=eps, scale=1.0 / (HEADS * HD)).then_inc(sem["mla_sd"], 1)

            def mla_round(k):
                act.wait_ge(sem["mla_a"], k + 1)
                copy(hid[:, HEADS + k, 0:FRAMES], mla_o[:, k, :]).then_inc(sem["mla_hi"], 1)

            for k in range(2):
                mla_round(k)
            ret_out(g)
            for k in range(2, 4):
                mla_round(k)
            ret_root(g)
            for k in range(4, HEADS):
                mla_round(k)
            ret_round(g)

            def wo_block(j, j0, more=0):
                wide_block(C_WO + j0, C_WO + j0, W_WO + j0, more)
                act.wait_ge(sem["acc_read"], C_WO + j0 + 1 + more)
                act.activation(sq[:], res[:, j, :], ACT.Square).then_inc(sem["h_sq"], 1)
                act.activation(xs[:, j, META:TOK], res[:, j, :], ACT.Identity,
                               scale=gain(G_MLP + j)).then_inc(sem["m_hi"], 1)

            with act.Fori(0, KT // 4) as i:
                for j in range(4):
                    wo_block(4 * i + j, j, 4 * i)

            for half in range(2):
                c0, b0, w0 = C_MLP + half * C_HALF, C_MLP + half * B_HALF, W_MLP + half * B_HALF

                def up(n, j0, more=0, root=False):
                    wide_block(c0 + j0, b0 + j0, w0 + j0, more)
                    if root:
                        act.wait_ge(sem["h_ss_ps"], 1)
                        act.activation(rstd[:], ps_x[:, 0:FRAMES], ACT.Sqrt, bias=eps, scale=1.0 / D).then_inc(sem["h_sd"], 1)
                    act.wait_ge(sem["up_r"], n + 1 + half * HALF_F)
                    act.activation(sq[:], r[:], ACT.Square).then_inc(sem["up_sq"], 1)
                    act.activation(hid[:, n, 0:FRAMES], r[:], ACT.Square).then_inc(sem["up_hi"], 1)

                if half == 1:
                    act.wait_ge(sem["dn_ss"], KT)
                for j in range(4):
                    up(j, j, root=half == 0 and j == 0)
                with act.Fori(1, HALF_F // 4) as i:
                    for j in range(4):
                        up(4 * i + j, j, 4 * i)

                cd, bd, wd = c0 + HALF_F, b0 + HALF_F, w0 + HALF_F

                def down(n, j0, more=0, ahead=True):
                    c = cd + 2 * j0
                    if ahead:
                        split_hi(c + 2, 0, more)
                        split_hi(c + 2, 1, more)
                    wide_block(c + 1, bd + j0, wd + j0, more, ahead)
                    act.wait_ge(sem["acc_read"], bd + n + 1)
                    if half == 1 and not ahead:
                        act.wait_ge(sem["dn_ss"], 2 * KT - 1)
                    act.activation(sq[:], res[:, n, :], ACT.Square).then_inc(sem["dn_sq"], 1)
                    if half == 1:
                        act.activation(res[:, n, :], res[:, n, :], ACT.Identity,
                                       scale=gain(G_FIN + n)).then_inc(sem["fin_g"], 1)

                with act.Fori(0, KT // 2 - 1) as i:
                    for j in range(2):
                        down(2 * i + j, j, 4 * i)
                down(KT - 2, 0, 4 * (KT // 2 - 1), True)
                down(KT - 1, 1, 4 * (KT // 2 - 1), half == 0)

            act.wait_ge(sem["fin_ps"], 1)
            act.activation(z[:], ps_x[:, 0:FRAMES], ACT.Sqrt, bias=eps, scale=1.0 / D).then_inc(sem["fin_sd"], 1)

        @block.vector
        def _(dve):
            def tt(o, a, b, op):
                return dve.tensor_tensor(o, a, b, op)

            def split_lo(c, part, more=0):
                if c >= C_END:
                    return
                dve.wait_ge(sem["hi_ready"], 2 * c + part + 1 + 2 * more)
                tt(halves(lo, c, part), raw_half(c, part), halves(hi, c, part).bitcast(F32),
                   ALU.subtract).then_inc(sem["lo_ready"], 1)

            def sum_ab(o, b, w, wmore=0):
                dve.wait_ge(sem["half_b"], w + 1 + wmore)
                return tt(o, acc[b % 2][:, 0:FRAMES], half_b[w % 2][:], ALU.add)

            def x_rest(k):
                dve.wait_ge(sem["x_hi"], k + 1)
                dve.scalar_tensor_tensor(out=xs[:, k, TOK:], in0=x_in[:, k, :], scalar=gain(G_MIX + k),
                                         in1=xs[:, k, 0:TOK].bitcast(F32), op0=ALU.mult,
                                         op1=ALU.subtract).then_inc(sem["x_lo"], 1)

            dve.wait_ge(sem["gains_landed"], 16)
            for k in range(3):
                dve.wait_ge(x_part[0], 16)
                x_rest(k)
            split_lo(0, 0)
            for k in range(3, 8):
                x_rest(k)
            split_lo(0, 1)
            for k in range(8, 16):
                x_rest(k)
            split_lo(1, 0)
            split_lo(1, 1)
            for c in range(2):
                split_lo(c + 2, 0)
                split_lo(c + 2, 1)
                dve.wait_ge(sem["chunk_used"], 2 * c + 2)
                dve.tensor_copy(ckv[:, c, :], acc[c % 2][:, 0:TOK]).then_inc(sem["acc_read"], 1)
            dve.wait_ge(sem["kv_sq"], 1)
            tt(kv_sq[:, 0, :], kv_sq[:, 0, :], kv_sq[:, 1, :], ALU.add).then_inc(sem["kv_sum"], 1)

            def side_rest(h):
                dve.wait_ge(sem["side_hi"], h + 1)
                tt(side_lo[:], side[:, 0:SIDE_V], side_hi[:].bitcast(F32), ALU.subtract).then_inc(sem["side_lo"], 1)

            def cq_block(k):
                split_lo(C_CQ + k + 2, 0)
                sum_ab(cq[:, k, :], C_CQ + k, k).then_inc(sem["acc_read"], 1)
                split_lo(C_CQ + k + 2, 1)
                dve.wait_ge(sem["cq_sq"], k + 1)
                if k == 0:
                    dve.tensor_copy(cq_ss[:], cq_sq[:, 0, :]).then_inc(sem["cq_sum"], 1)
                else:
                    dve.wait_ge(sem["cq_sum"], k)
                    tt(cq_ss[:], cq_ss[:], cq_sq[:, k, :], ALU.add).then_inc(sem["cq_sum"], 1)
                dve.wait_ge(sem["cq_hi"], k + 1)
                dve.scalar_tensor_tensor(out=cqs[:, k, FRAMES:], in0=cq[:, k, :], scalar=gain(G_Q + k),
                                         in1=cqs[:, k, 0:FRAMES].bitcast(F32), op0=ALU.mult,
                                         op1=ALU.subtract).then_inc(sem["cq_lo"], 1)

            cq_block(0)
            cq_block(1)
            dve.wait_ge(sem["rx_sd"], 1)
            dve.reciprocal(rstdx[:], rx_sd[:]).then_inc(sem["rstdx"], 1)
            dve.wait_ge(sem["rstdx"], 1)
            tt(rstdx2[:], rstdx[:], rstdx[:], ALU.mult).then_inc(sem["stat"], 1)
            dve.wait_ge(sem["stat"], 1)
            dve.wait_ge(sem["ss_k_ps"], 1)
            tt(kv_var[:], ps_v[:, 0:TOK], rstdx2[:], ALU.mult).then_inc(sem["kv_var"], 1)
            dve.wait_ge(sem["kv_sd"], 1)
            dve.reciprocal(kv_var[:], kv_f[:]).then_inc(sem["stat"], 1)
            dve.wait_ge(sem["stat"], 2)
            tt(kv_f[:], kv_var[:], rstdx[:], ALU.mult).then_inc(sem["stat"], 1)
            dve.wait_ge(sem["stat"], 3)
            for k in range(KVL // P):
                dve.scalar_tensor_tensor(out=ckv[:, k, :], in0=ckv[:, k, :], scalar=gain(G_KV + k), in1=kv_f[:],
                                         op0=ALU.mult, op1=ALU.mult).then_inc(sem["kv_scaled"], 1)
            cq_block(2)
            dve.wait_ge(sem["kv_hi"], 1)
            tt(ckvs[:, :, TOK:], ckv[:], ckvs[:, :, 0:TOK].bitcast(F32), ALU.subtract).then_inc(sem["kv_lo"], 1)
            dve.wait_ge(sem["consts_landed"], 16)
            tt(cos_r, cos_r, rstdx[:], ALU.mult).then_inc(sem["tables"], 1)
            tt(sin_r, sin_r, rstdx[:], ALU.mult).then_inc(sem["tables"], 1)
            cq_block(3)
            split_lo(8, 0)
            dve.wait_ge(sem["acc_read"], C_KR + 1)
            tt(kr[0:ROPE, :], zk[0:ROPE, :], consts[0:ROPE, K_COSM:K_COSM + TOK], ALU.mult).then_inc(sem["kr_raw"], 1)
            tt(kr_v[0:ROPE, :], zk[ROPE:, :], consts[ROPE:, K_SINM:K_SINM + TOK], ALU.mult).then_inc(sem["kr_raw"], 1)
            dve.wait_ge(sem["kr_raw"], 2)
            tt(kr[0:ROPE, :], kr[0:ROPE, :], kr_v[0:ROPE, :], ALU.add).then_inc(sem["kr_raw"], 1)
            dve.wait_ge(sem["kr_raw"], 3)
            tt(kr[0:ROPE, :], kr[0:ROPE, :], rstdx[0:ROPE, :], ALU.mult).then_inc(sem["kr_ready"], 1)
            split_lo(8, 1)
            dve.wait_ge(sem["ss_q_ps"], 1)
            tt(cq_var[:], ps_y[:, 0:FRAMES], rstdx2[:, META:], ALU.mult).then_inc(sem["cq_var"], 1)
            side_rest(0)
            dve.wait_ge(sem["cq_sd"], 1)
            dve.reciprocal(cq_var[:], cq_sd[:]).then_inc(sem["stat"], 1)
            dve.wait_ge(sem["stat"], 4)
            tt(q_rstd[:], cq_var[:], rstdx[:, META:], ALU.mult).then_inc(sem["stat"], 1)
            dve.wait_ge(sem["stat"], 5)
            tt(cos_q, cos_q, q_rstd[0:ROPE, :], ALU.mult).then_inc(sem["tables"], 1)
            tt(sin_q, sin_q, q_rstd[ROPE:, :], ALU.mult).then_inc(sem["tables"], 1)

            def q_sum(h, c, w, m, wm):
                split_lo(c + 2, 0, m)
                sum_ab(zq[:], c, w, wm).then_inc(sem["acc_read"], 1)
                split_lo(c + 2, 1, m)

            def q_rope(h):
                dve.wait_ge(sem["rq_sw"], 2 * h + 2)
                tt(swq[:], swq[:], sin_r[:, META:], ALU.mult).then_inc(sem["rq_sin"], 1)
                dve.wait_ge(sem["rq_sin"], h + 1)
                dve.wait_ge(sem["rq_cos"], h + 1)
                tt(rq[:], rq[:], swq[:], ALU.add).then_inc(sem["rq_ready"], 1)

            def k_rope(h, c, m):
                split_lo(c + 2, 0, m)
                dve.wait_ge(sem["acc_read"], c + 1 + m)
                tt(swk[:], swk[:], sin_r, ALU.mult).then_inc(sem["rk_sin"], 1)
                split_lo(c + 2, 1, m)
                dve.wait_ge(sem["rk_sin"], h + 1)
                dve.wait_ge(sem["rk_cos"], h + 1)
                tt(rk[:], rk[:], swk[:], ALU.add).then_inc(sem["rk_ready"], 1)

            def v_norm(h, c, m):
                split_lo(c + 2, 0, m)
                dve.wait_ge(sem["chunk_used"], 2 * c + 2 + 2 * m)
                tt(rv[:], acc[c % 2][:, 0:TOK], rstdx[:], ALU.mult).then_inc(sem["acc_read"], 1)
                split_lo(c + 2, 1, m)

            def mla_in(h):
                dve.wait_ge(sem["qn_b"], h + 1)
                tt(qn[:], ps_qn[:, 0:FRAMES], qn_b[:], ALU.add).then_inc(sem["qn_raw"], 1)
                dve.wait_ge(sem["qr_b"], h + 1)
                tt(qr_z[:], ps_qr[:, 0:FRAMES], qr_b[:], ALU.add).then_inc(sem["qr_raw"], 1)
                dve.wait_ge(sem["kn_ps"], h + 1)
                dve.tensor_copy(kn[:], ps_kn[:, 0:TOK]).then_inc(sem["kn_ready"], 1)
                dve.wait_ge(sem["qn_raw"], h + 1)
                tt(qn[:], qn[:], q_rstd[:], ALU.mult).then_inc(sem["qn_ready"], 1)
                dve.wait_ge(sem["qr_raw"], h + 1)
                tt(qr_v[0:ROPE, :], qr_z[ROPE:, :], sin_q, ALU.mult).then_inc(sem["qr_u"], 1)
                dve.wait_ge(sem["qr_u"], 2 * h + 2)
                tt(qr[0:ROPE, :], qr[0:ROPE, :], qr_v[0:ROPE, :], ALU.add).then_inc(sem["qr_ready"], 1)

            def mla_softmax(h):
                dve.wait_ge(sem["mla_s_ps"], h + 1)
                dve.scalar_tensor_tensor(out=probs[:], in0=ps_qn[:, 0:SCORES], scalar=float((NOPE + ROPE) ** -0.5),
                                         in1=mask, op0=ALU.mult, op1=ALU.add).then_inc(sem["mla_s"], 1)
                dve.wait_ge(sem["mla_s"], h + 1)
                for n, (c0, keys) in enumerate(((0, Q0K), (Q0K, Q1K))):
                    dve.tensor_reduce(stats[:, n:n + 1], probs[:, c0:c0 + keys], AX.X, ALU.max,
                                      negate=True).then_inc(sem["mla_max"], 1)

            def mla_norm(h):
                dve.wait_ge(sem["mla_exp"], 2 * h + 2)
                dve.reciprocal(stats[:, 4:6], stats[:, 2:4]).then_inc(sem["mla_inv"], 1)
                dve.wait_ge(sem["mla_inv"], h + 1)
                for n, (c0, keys) in enumerate(((0, Q0K), (Q0K, Q1K))):
                    dve.tensor_scalar(probs[:, c0:c0 + keys], probs[:, c0:c0 + keys], stats[:, 4 + n:5 + n], None,
                                      ALU.mult).then_inc(sem["mla_p"], 1)

            def mla_turned(h):
                dve.wait_ge(sem["pt_ps"], h + 1)
                dve.tensor_copy(pt_f[:].rearrange("p a t -> p (a t)"), ps_kn[:, 0:3 * P]).then_inc(sem["pt_f"], 1)

            def mla_out(h):
                dve.wait_ge(sem["mla_o_ps"], h + 1)
                dve.tensor_copy(mla_o[:, h, :], ps_qn[:, 0:FRAMES]).then_inc(sem["mla_o"], 1)

            def ret_in(g):
                dve.wait_ge(sem["decay"], g + 1)
                dve.wait_ge(sem["ret_s_ps"], g + 1)
                scale = float(HD ** -0.5)

                def decayed(o, i, d):
                    dve.scalar_tensor_tensor(out=o, in0=i, scalar=scale, in1=d, op0=ALU.mult,
                                             op1=ALU.mult).then_inc(sem["ret_s"], 1)

                decayed(ret_s[:, 0:FRAMES], ps_x[:, 0:FRAMES], decay[:, 0:FRAMES])
                decayed(ret_s[0:META, FRAMES + P:], ps_x[0:META, FRAMES:], decay[0:META, FRAMES + P:])
                dve.wait_ge(sem["ret_y_ps"], g + 1)
                decayed(ret_s[:, FRAMES:FRAMES + P], ps_y[:, 0:P], decay[:, FRAMES:FRAMES + P])
                dve.tensor_copy(ret_v[0:META, 0, :], ps_y[0:META, P:2 * P]).then_inc(sem["ret_v"], 1)
                dve.tensor_copy(ret_v[:, 1:3, :].rearrange("p a t -> p (a t)"), ps_y[:, 2 * P:]).then_inc(sem["ret_v"], 1)

            def ret_norm(g):
                dve.wait_ge(sem["ret_sd"], g + 1)
                dve.reciprocal(r[:], z[:]).then_inc(sem["ret_inv"], 1)
                dve.wait_ge(sem["ret_inv"], g + 1)
                tt(r[:], cen[:], r[:], ALU.mult).then_inc(sem["ret_y"], 1)
                dve.wait_ge(sem["ret_y"], g + 1)
                dve.wait_ge(sem["gate"], g + 1)
                dve.scalar_tensor_tensor(out=cen[:], in0=r[:], scalar=gain(G_RET + g), in1=gate[:], op0=ALU.mult,
                                         op1=ALU.mult).then_inc(sem["ret_a"], 1)

            def ret_rest(g):
                dve.wait_ge(sem["ret_hi"], g + 1)
                tt(hid[:, g, FRAMES:], cen[:], hid[:, g, 0:FRAMES].bitcast(F32), ALU.subtract).then_inc(sem["ret_lo"], 1)

            def gate_sum(g, c, w, m, wm):
                split_lo(c + 2, 0, m)
                sum_ab(gate_z[:], c, w, wm).then_inc(sem["acc_read"], 1)
                split_lo(c + 2, 1, m)

            def gate_inv(g):
                dve.wait_ge(sem["gate_exp"], g + 1)
                dve.tensor_scalar(gate[:], gate[:], 1.0, None, ALU.add).then_inc(sem["gate_den"], 1)
                dve.wait_ge(sem["gate_den"], g + 1)
                dve.reciprocal(gate[:], gate[:]).then_inc(sem["gate_inv"], 1)

            q_sum(0, C_HEAD0, W_HEAD0, 0, 0)
            mla_in(0)
            q_rope(0)
            k_rope(0, C_HEAD0 + 1, 0)
            mla_softmax(0)
            mla_norm(0)
            v_norm(0, C_HEAD0 + 2, 0)
            mla_turned(0)
            mla_out(0)
            side_rest(1)

            def head(h, i, last=False):
                c, m = C_HEAD, 4 * i
                gate_sum(h - 1, c, W_HEAD, m, 2 * i)
                mla_in(h)
                ret_in(h - 1)
                gate_inv(h - 1)
                q_sum(h, c + 1, W_HEAD + 1, m, 2 * i)
                mla_softmax(h)
                q_rope(h)
                mla_norm(h)
                k_rope(h, c + 2, m)
                mla_turned(h)
                if not last:
                    side_rest(h + 1)
                ret_norm(h - 1)
                v_norm(h, c + 3, m)
                mla_out(h)
                ret_rest(h - 1)

            with dve.Fori(0, HEADS - 2) as i:
                head(i + 1, i)
            head(HEADS - 1, HEADS - 2, last=True)

            g = HEADS - 1
            gate_sum(g, C_GATE7, W_GATE7, 0, 0)
            ret_in(g)
            dve.wait_ge(sem["mla_sd"], 1)
            dve.reciprocal(rstd[:], rstd[:]).then_inc(sem["mla_rstd"], 1)
            dve.wait_ge(sem["mla_rstd"], 1)

            def mla_scale(k):
                dve.scalar_tensor_tensor(out=mla_o[:, k, :], in0=mla_o[:, k, :], scalar=gain(G_MLA + k), in1=rstd[:],
                                         op0=ALU.mult, op1=ALU.mult).then_inc(sem["mla_a"], 1)

            def mla_rest(k):
                dve.wait_ge(sem["mla_hi"], k + 1)
                tt(hid[:, HEADS + k, FRAMES:], mla_o[:, k, :], hid[:, HEADS + k, 0:FRAMES].bitcast(F32),
                   ALU.subtract).then_inc(sem["mla_lo"], 1)

            for k in range(4):
                mla_scale(k)
            for k in range(4):
                mla_rest(k)
            gate_inv(g)
            for k in range(4, HEADS):
                mla_scale(k)
            mla_rest(4)
            mla_rest(5)
            ret_norm(g)
            mla_rest(6)
            mla_rest(7)
            ret_rest(g)

            def residual(n, b, res_ready):
                dve.wait_ge(res_ready[0], res_ready[1])
                tt(res[:, n, :], acc[b % 2][:, 0:FRAMES], t2[:], ALU.add).then_inc(sem["acc_read"], 1)

            def wo_block(j, j0, m=0):
                split_lo(C_WO + j0 + 2, 0, m)
                residual(j, C_WO + j0, (sem["wo_res"], j + 1))
                split_lo(C_WO + j0 + 2, 1, m)
                dve.wait_ge(sem["m_hi"], j + 1)
                dve.scalar_tensor_tensor(out=xs[:, j, TOK + META:], in0=res[:, j, :], scalar=gain(G_MLP + j),
                                         in1=xs[:, j, META:TOK].bitcast(F32), op0=ALU.mult,
                                         op1=ALU.subtract).then_inc(sem["m_lo"], 1)

            with dve.Fori(0, KT // 4) as i:
                for j in range(4):
                    wo_block(4 * i + j, j, 4 * i)

            for half in range(2):
                c0, b0, w0 = C_MLP + half * C_HALF, C_MLP + half * B_HALF, W_MLP + half * B_HALF

                def up(n, j0, m=0, root=False):
                    split_lo(c0 + j0 + 2, 0, m)
                    sum_ab(z[:], b0 + j0, w0 + j0, m).then_inc(sem["acc_read"], 1)
                    if root:
                        dve.wait_ge(sem["h_sd"], 1)
                        dve.reciprocal(rstd[:], rstd[:]).then_inc(sem["h_rstd"], 1)
                        dve.wait_ge(sem["h_rstd"], 1)
                    dve.wait_ge(sem["acc_read"], b0 + j0 + 1 + m)
                    dve.scalar_tensor_tensor(out=r[:], in0=z[:], scalar=0.0, in1=rstd[:], op0=ALU.max,
                                             op1=ALU.mult).then_inc(sem["up_r"], 1)
                    split_lo(c0 + j0 + 2, 1, m)
                    dve.wait_ge(sem["up_hi"], n + 1 + half * HALF_F)
                    tt(hid[:, n, FRAMES:], sq[:], hid[:, n, 0:FRAMES].bitcast(F32), ALU.subtract).then_inc(sem["up_lo"], 1)

                for j in range(4):
                    up(j, j, root=half == 0 and j == 0)
                with dve.Fori(1, HALF_F // 4) as i:
                    for j in range(4):
                        up(4 * i + j, j, 4 * i)

                cd, bd = c0 + HALF_F, b0 + HALF_F

                def down(n, j0, m=0, ahead=True):
                    c = cd + 2 * j0
                    if ahead:
                        split_lo(c + 2, 0, m)
                        split_lo(c + 2, 1, m)
                        split_lo(c + 3, 0, m)
                    if half == 1 and not ahead:
                        sum_ab(t2[:], bd + j0, W_MLP + 2 * B_HALF - 1).then_inc(sem["last_a"], 1)
                        dve.wait_ge(sem["last_a"], 1)
                        tt(res[:, n, :], t2[:], res[:, n, :], ALU.add).then_inc(sem["acc_read"], 1)
                    else:
                        residual(n, bd + j0, (sem["dn_res"], n + 1 + half * KT))
                    if ahead:
                        split_lo(c + 3, 1, m)

                with dve.Fori(0, KT // 2 - 1) as i:
                    for j in range(2):
                        down(2 * i + j, j, 4 * i)
                down(KT - 2, 0, 4 * (KT // 2 - 1), True)
                down(KT - 1, 1, 4 * (KT // 2 - 1), half == 0)

            dve.wait_ge(sem["fin_sd"], 1)
            dve.reciprocal(rstd[:], z[:]).then_inc(sem["fin_rstd"], 1)
            dve.wait_ge(sem["fin_rstd"], 1)
            dve.wait_ge(sem["fin_g"], KT)
            for k in range(KT):
                if k % 4 != 3:
                    tt(res[:, k, :], res[:, k, :], rstd[:], ALU.mult).then_inc(sem["fin_out"], 1)

        @block.gpsimd
        def _(pool):
            def tt(o, a, b, op):
                return pool.tensor_tensor(o, a, b, op)

            pool.memset(v_sb[:, 0, :], 0.0).then_inc(sem["meta_pad"], 1)
            pool.memset(pt_m[:], 0.0).then_inc(sem["meta_pad"], 1)
            pool.memset(ret_s[:, FRAMES + P:], 0.0).then_inc(sem["meta_pad"], 1)
            pool.memset(sum_sq[:], 0.0).then_inc(sem["meta_pad"], 1)
            for n in range(4):
                pool.wait_ge(x_part[n], 16)
            tt(x_sq[:], x_in[:], x_in[:], ALU.mult).then_inc(sem["ssx"], 1)
            n = KT // 2
            step = 1
            while n:
                pool.wait_ge(sem["ssx"], step)
                tt(x_sq[:, 0:n, :], x_sq[:, 0:n, :], x_sq[:, n:2 * n, :], ALU.add).then_inc(sem["ssx"], 1)
                n //= 2
                step += 1

            def q_cos(h, c, m):
                pool.wait_ge(sem["acc_read"], c + 1 + m)
                tt(rq[:], zq[:], cos_r[:, META:], ALU.mult).then_inc(sem["rq_cos"], 1)

            def k_cos(h, c, m):
                pool.wait_ge(sem["acc_read"], c + 1 + m)
                tt(rk[:], zk[:], cos_r, ALU.mult).then_inc(sem["rk_cos"], 1)

            def qr_cos(h):
                pool.wait_ge(sem["qr_raw"], h + 1)
                tt(qr[0:ROPE, :], qr_z[0:ROPE, :], cos_q, ALU.mult).then_inc(sem["qr_u"], 1)

            def mla_sum(h):
                pool.wait_ge(sem["mla_sq"], h + 1)
                tt(sum_sq[:], sum_sq[:], t2[:], ALU.add).then_inc(sem["mla_ss"], 1)

            def gate_norm(g, c, m):
                pool.wait_ge(sem["acc_read"], c + 1 + m)
                tt(gate_z[:], gate_z[:], rstdx[:, META:], ALU.mult).then_inc(sem["gate_z"], 1)

            def gate_mul(g):
                pool.wait_ge(sem["gate_inv"], g + 1)
                tt(gate[:], gate_z[:], gate[:], ALU.mult).then_inc(sem["gate"], 1)

            pool.wait_ge(sem["cq_lo"], QL // P)
            pool.memset(ret_v[:, 0, :], 0.0).then_inc(sem["meta_pad"], 1)
            pool.wait_ge(sem["tables"], 2)
            q_cos(0, C_HEAD0, 0)
            pool.wait_ge(sem["tables"], 4)
            qr_cos(0)
            k_cos(0, C_HEAD0 + 1, 0)
            pool.wait_ge(sem["meta_pad"], 5)
            mla_sum(0)
            with pool.Fori(0, HEADS - 1) as i:
                c, m, h = C_HEAD, 4 * i, i + 1
                gate_norm(h - 1, c, m)
                qr_cos(h)
                gate_mul(h - 1)
                q_cos(h, c + 1, m)
                k_cos(h, c + 2, m)
                mla_sum(h)
            gate_norm(HEADS - 1, C_GATE7, 0)
            gate_mul(HEADS - 1)

            def res_sum(n, w, wm, done):
                pool.wait_ge(sem["half_b"], w + 1 + wm)
                tt(t2[:], half_b[w % 2][:], res[:, n, :], ALU.add).then_inc(done, 1)

            pool.wait_ge(sem["mla_ss_ps"], 1)
            pool.memset(sum_sq[:], 0.0).then_inc(sem["meta_pad"], 1)
            pool.wait_ge(sem["meta_pad"], 6)
            pool.wait_ge(sem["x_back"], 16)
            with pool.Fori(0, KT // 4) as i:
                for j in range(4):
                    res_sum(4 * i + j, W_WO + j, 4 * i, sem["wo_res"])
                    pool.wait_ge(sem["h_sq"], 4 * i + j + 1)
                    tt(sum_sq[:], sum_sq[:], sq[:], ALU.add).then_inc(sem["h_ss"], 1)
            for half in range(2):
                w0 = W_MLP + half * B_HALF + HALF_F
                pool.wait_ge(sem["h_ss_ps"] if half == 0 else sem["dn_ss"], 1 if half == 0 else KT)
                pool.memset(sum_sq[:], 0.0).then_inc(sem["meta_pad"], 1)
                pool.wait_ge(sem["meta_pad"], 7 + half)

                def down(n, w, wm, last=False):
                    if not last:
                        res_sum(n, w, wm, sem["dn_res"])
                        pool.wait_ge(sem["dn_sq"], n + 1 + half * KT)
                        tt(sum_sq[:], sum_sq[:], sq[:], ALU.add).then_inc(sem["dn_ss"], 1)

                with pool.Fori(0, KT // 2 - 1) as i:
                    for j in range(2):
                        down(2 * i + j, w0 + j, 2 * i)
                down(KT - 2, w0 + KT - 2, 0)
                down(KT - 1, w0 + KT - 1, 0, half == 1)
            pool.wait_ge(sem["fin_rstd"], 1)
            pool.wait_ge(sem["fin_g"], KT)
            for k in range(3, KT, 4):
                tt(res[:, k, :], res[:, k, :], rstd[:], ALU.mult).then_inc(sem["fin_pool"], 1)


def constants():
    f = np.float32
    c = np.zeros((P, K_END), f)
    c[:, K_ID:K_ID + P] = np.eye(P)
    c[:, K_CEN:K_CEN + P] = np.eye(P) - 1.0 / P
    c[:, K_ONE:K_ONE + P] = 1.0
    frame = np.arange(FRAMES)
    meta = np.arange(-META, 0)

    def distance(keys, queries):
        k, q = keys[:, None], queries[None, :]
        seen = k // CHUNK <= q // CHUNK
        return np.where(seen, np.abs(q - k), 1e6).astype(f)

    c[:, K_DIST:K_DIST + FRAMES] = distance(frame[:P], frame)
    c[:, K_DIST + FRAMES:K_DIST + FRAMES + P] = distance(frame[P:], frame[P:])
    c[:META, K_DIST + FRAMES + P:K_DIST + 640] = distance(meta, frame)
    tokens = np.concatenate([meta, frame])

    def additive(queries, keys):
        seen = keys[None, :] // CHUNK <= queries[:, None] // CHUNK
        return np.where(seen, 0.0, -3e38).astype(f)

    c[:, K_MASK:K_MASK + Q0K] = additive(frame[:P], tokens[:Q0K])
    c[:, K_MASK + Q0K:K_MASK + SCORES] = additive(frame[P:], tokens)
    c[:, K_LG:K_LG + HEADS] = np.log(f(1) - f(2) ** (f(-5) - np.arange(HEADS, dtype=f)))[None]
    pos = np.arange(TOK, dtype=f)

    def angles(dim):
        inv = f(1) / (f(10000.0) ** (np.arange(0, dim, 2, dtype=f) / f(dim)))
        return (pos[:, None] * inv[None, :]).astype(f).T

    a = angles(HD)
    c[:, K_COSR:K_COSR + TOK] = np.concatenate([np.cos(a), np.cos(a)])
    c[:, K_SINR:K_SINR + TOK] = np.concatenate([-np.sin(a), np.sin(a)])
    a = angles(ROPE)
    c[:, K_COSM:K_COSM + TOK] = np.concatenate([np.cos(a)] * 4)
    c[:, K_SINM:K_SINM + TOK] = np.concatenate([-np.sin(a), np.sin(a)] * 2)
    c[:, K_EPS] = EPS
    return c


def blocks(w):
    k, n = w.shape
    return w.reshape(k // P, P, n // P, P).transpose(2, 1, 0, 3).reshape(n // P, P, k)


def rows(w):
    return w.reshape(-1, P, w.shape[1]).transpose(1, 0, 2)


def swapped(w):
    return np.concatenate([w[:, w.shape[1] // 2:], w[:, :w.shape[1] // 2]], 1)


def kernel(x, meta_tokens, norm_mix_g, w_in, ret_out_g, q_norm_g, w_uq, kv_norm_g, w_uk, w_uv, mla_out_g, w_o,
           norm_mlp_g, w_up, w_down, final_norm_g):
    import concourse.bacc as bacc
    from concourse.bass_utils import run_bass_kernel_spmd as run

    a = np.asarray
    w = a(w_in)[0]
    ends = np.cumsum([HEADS * HD] * 4 + [QL, KVL, ROPE])
    wq, wk, wv, wg, wcq, wckv, wkr = np.split(w, ends[:-1], axis=1)
    bq, bk, bv, bg = (blocks(m) for m in (wq, wk, wv, wg))
    order = [blocks(wckv), blocks(wcq), blocks(np.concatenate([wkr, swapped(wkr)], 1)), bq[0:1], bk[0:1], bv[0:1]]
    for h in range(1, HEADS):
        order += [bg[h - 1:h], bq[h:h + 1], bk[h:h + 1], bv[h:h + 1]]
    stream_in = np.concatenate(order + [bg[HEADS - 1:]])

    uq = a(w_uq)[0].reshape(QL, HEADS, NOPE + ROPE)
    uk = a(w_uk)[0].reshape(KVL, HEADS, NOPE)
    uv = a(w_uv)[0].reshape(KVL, HEADS, HD)

    def side_of(h):
        rot = uq[:, h, NOPE:]
        parts = [uq[:, h, :NOPE], np.concatenate([rot, swapped(rot)], 1), uk[:, h], uv[:, h]]
        return np.concatenate([rows(m).reshape(P, -1) for m in parts], 1)

    side = np.stack([side_of(h) for h in range(HEADS)])
    up = blocks(a(w_up)[0])
    half = DFF // 2
    down = a(w_down)[0].reshape(2, DOWN_PER_BLOCK, D, D)
    down = np.stack([np.stack([blocks(down[i, j]) for j in range(DOWN_PER_BLOCK)], 1) for i in range(2)])
    down = down.reshape(-1, P, W)
    frames = rows(a(x)[0].T)
    tokens = np.concatenate([rows(a(meta_tokens).T), frames], 2)
    g = [a(norm_mix_g)[0], a(q_norm_g)[0], a(kv_norm_g)[0], a(ret_out_g)[0], a(mla_out_g)[0], a(norm_mlp_g)[0],
         a(final_norm_g)]
    gains = np.concatenate([v.reshape(-1, P).T for v in g], 1)

    ins = {"w_in": stream_in, "w_side": side, "w_o": blocks(a(w_o)[0].reshape(KT, P, D)[WO_ORDER].reshape(D, D)), "w_up": up, "w_down": down,
           "x_all": tokens, "x_frames": frames, "gains_in": gains, "consts_in": constants()}
    ins = {n: np.ascontiguousarray(v) for n, v in ins.items()}
    nc = bacc.Bacc("TRN2", target_bir_lowering=False, num_devices=1)
    aps = {n: nc.dram_tensor(n, v.shape, mybir.dt.from_np(v.dtype), kind="ExternalInput").ap() for n, v in ins.items()}
    aps["out"] = nc.dram_tensor("out", (P, KT, FRAMES), F32, kind="ExternalOutput").ap()
    hymba_block(nc, **aps)
    got = run(nc, [ins], core_ids=[0]).results[0]["out"]
    return got.transpose(1, 0, 2).reshape(D, FRAMES).T.reshape(1, FRAMES, D)
```
